# Optimizing a Trainium2 kernel written in Bass

```python
import jax, jax.numpy as jnp
from jax import lax
import numpy as np

D_MODEL = 1024
BATCH = 1
SEQ = 512
DEPTH = 2
DEC_BATCH = 8
DEC_SEQ = 16
PAST_LEN = 512

CHUNK = 64
MIX_WIDTH = D_MODEL
RET_HEADS = 4
RET_HEAD_DIM = 64
RET_WIDTH = RET_HEADS * RET_HEAD_DIM
FOX_HEADS = 8
FOX_HEAD_DIM = 64
FOX_WIDTH = FOX_HEADS * FOX_HEAD_DIM
CONV_DIM = MIX_WIDTH - RET_WIDTH - FOX_WIDTH
CONV_W = 3
FFN_CONV_W = 3
D_FF = 256 * ((8 * D_MODEL // 3 + 255) // 256)
FOX_QBLOCK = 128
ROPE_BASE = 10000.0
NORM_EPS = 1e-6
PROJ_SIZES = (RET_WIDTH,) * 4 + (FOX_WIDTH,) * 3 + (FOX_HEADS,) + (CONV_DIM,) * 3
PROJ_DIM = sum(PROJ_SIZES)

kernel_name = "hybrid_streaming_retention_fox_conv"

def _rms_norm(x, g):
    xf = x.astype(jnp.float32)
    y = xf * lax.rsqrt(jnp.mean(xf * xf, axis=-1, keepdims=True) + NORM_EPS)
    return (y * g.astype(jnp.float32)).astype(x.dtype)

def _head_group_norm(o, g):
    mu = jnp.mean(o, axis=-1, keepdims=True)
    d = o - mu
    return d * lax.rsqrt(jnp.mean(d * d, axis=-1, keepdims=True) + NORM_EPS) * g.astype(jnp.float32)

def _rotary(x, pos):
    half = x.shape[-1] // 2
    inv_freq = ROPE_BASE ** (-jnp.arange(half, dtype=jnp.float32) / half)
    ang = pos.astype(jnp.float32)[:, None] * inv_freq[None, :]
    cos = jnp.cos(ang)[None, :, None, :]
    sin = jnp.sin(ang)[None, :, None, :]
    xf = x.astype(jnp.float32)
    x1, x2 = xf[..., :half], xf[..., half:]
    return jnp.concatenate([x1 * cos - x2 * sin, x1 * sin + x2 * cos], axis=-1).astype(x.dtype)

def _causal_dwconv(u, hist, w):
    width = w.shape[0]
    s = u.shape[1]
    full = jnp.concatenate([hist.astype(u.dtype), u], axis=1)
    y = full[:, 0:s] * w[0]
    for j in range(1, width):
        y = y + full[:, j:j + s] * w[j]
    return y.astype(u.dtype), full[:, s:]

def _retention(q, k, v, s0):
    L = q.shape[2]
    log_g = jnp.log1p(-jnp.exp2(-5.0 - jnp.arange(RET_HEADS, dtype=jnp.float32)))
    i = jnp.arange(L, dtype=jnp.float32)
    diff = i[:, None] - i[None, :]
    decay = jnp.where(diff[None] >= 0.0,
                      jnp.exp(jnp.maximum(diff, 0.0)[None] * log_g[:, None, None]), 0.0)
    scores = jnp.einsum('bcihd,bcjhd->bchij', q, k) * decay
    o_inner = jnp.einsum('bchij,bcjhe->bcihe', scores, v)
    k_w = k * jnp.exp((L - 1.0 - i)[:, None] * log_g[None, :])[:, :, None]
    ds = jnp.einsum('bcjhd,bcjhe->bchde', k_w, v)
    g_block = jnp.exp(L * log_g)[:, None, None]

    def step(s, ds_c):
        return g_block * s + ds_c, s

    s_fin, s_prev = lax.scan(step, s0, jnp.moveaxis(ds, 1, 0))
    s_prev = jnp.moveaxis(s_prev, 0, 1)
    q_w = q * jnp.exp((i + 1.0)[:, None] * log_g[None, :])[:, :, None]
    o_cross = jnp.einsum('bcihd,bchde->bcihe', q_w, s_prev)
    return o_inner + o_cross, s_fin

def _fox_prompt(q, k, v, logf):
    b, s, h, d = q.shape
    nb = s // FOX_QBLOCK
    scale = d ** -0.5
    c_t = jnp.transpose(jnp.cumsum(logf, axis=1), (0, 2, 1))
    kpos = jnp.arange(s)
    qb = jnp.moveaxis(q.reshape(b, nb, FOX_QBLOCK, h, d), 1, 0)
    cqb = jnp.moveaxis(c_t.reshape(b, h, nb, FOX_QBLOCK), 2, 0)
    qpos = kpos.reshape(nb, FOX_QBLOCK)

    def block(args):
        qi, cqi, pi = args
        sc = jnp.einsum('bqhd,bkhd->bhqk', qi, k, preferred_element_type=jnp.float32) * scale
        sc = sc + cqi[..., None] - c_t[:, :, None, :]
        sc = jnp.where(kpos[None, :] <= pi[:, None], sc, -jnp.inf)
        p = jax.nn.softmax(sc, axis=-1)
        return jnp.einsum('bhqk,bkhd->bqhd', p.astype(v.dtype), v)

    o = lax.map(block, (qb, cqb, qpos))
    return jnp.moveaxis(o, 0, 1).reshape(b, s, h, d)

def _fox_sample(q, k, v, logf, ck, cv, clogf):
    p_len = ck.shape[1]
    n = q.shape[1]
    scale = q.shape[-1] ** -0.5
    k_all = jnp.concatenate([ck.astype(k.dtype), k], axis=1)
    v_all = jnp.concatenate([cv.astype(v.dtype), v], axis=1)
    lf_all = jnp.concatenate([clogf.astype(jnp.float32), logf], axis=1)
    c_t = jnp.transpose(jnp.cumsum(lf_all, axis=1), (0, 2, 1))
    cq = c_t[:, :, p_len:]
    sc = jnp.einsum('bqhd,bkhd->bhqk', q, k_all, preferred_element_type=jnp.float32) * scale
    sc = sc + cq[..., None] - c_t[:, :, None, :]
    mask = jnp.arange(p_len + n)[None, :] <= (p_len + jnp.arange(n))[:, None]
    sc = jnp.where(mask, sc, -jnp.inf)
    p = jax.nn.softmax(sc, axis=-1)
    return jnp.einsum('bhqk,bkhd->bqhd', p.astype(v_all.dtype), v_all)

def _layer(x, pos, hist, prm, prompt):
    (norm_mix, w_in, ret_gn_gain, fox_q_gain, fox_k_gain, fox_f_bias, conv_w,
     w_out, norm_ffn, w_gate, w_up, ffn_conv_w, w_down) = prm
    f32 = jnp.float32
    b, s, _ = x.shape
    h = _rms_norm(x, norm_mix)
    proj = h @ w_in
    split_at = np.cumsum(PROJ_SIZES)[:-1].tolist()
    rq, rk, rv, rg, fq, fk, fv, fl, cb, cc, ch = jnp.split(proj, split_at, axis=-1)

    q = _rotary(rq.reshape(b, s, RET_HEADS, RET_HEAD_DIM), pos).astype(f32)
    k = _rotary(rk.reshape(b, s, RET_HEADS, RET_HEAD_DIM), pos).astype(f32) * RET_HEAD_DIM ** -0.5
    v = rv.reshape(b, s, RET_HEADS, RET_HEAD_DIM).astype(f32)
    if prompt:
        n_c = s // CHUNK
        s0 = jnp.zeros((b, RET_HEADS, RET_HEAD_DIM, RET_HEAD_DIM), f32)
    else:
        n_c = 1
        s0 = hist[3].astype(f32)
    blk = lambda t: t.reshape(b, n_c, s // n_c, RET_HEADS, RET_HEAD_DIM)
    o_ret, ret_state = _retention(blk(q), blk(k), blk(v), s0)
    o_ret = _head_group_norm(o_ret.reshape(b, s, RET_HEADS, RET_HEAD_DIM),
                             ret_gn_gain.reshape(RET_HEADS, RET_HEAD_DIM))
    o_ret = (o_ret.reshape(b, s, RET_WIDTH) * jax.nn.silu(rg.astype(f32))).astype(x.dtype)

    fqh = _rms_norm(fq.reshape(b, s, FOX_HEADS, FOX_HEAD_DIM), fox_q_gain)
    fkh = _rms_norm(fk.reshape(b, s, FOX_HEADS, FOX_HEAD_DIM), fox_k_gain)
    fvh = fv.reshape(b, s, FOX_HEADS, FOX_HEAD_DIM)
    logf = jax.nn.log_sigmoid(fl.astype(f32) + fox_f_bias.astype(f32))
    if prompt:
        o_fox = _fox_prompt(fqh, fkh, fvh, logf)
    else:
        o_fox = _fox_sample(fqh, fkh, fvh, logf, hist[0], hist[1], hist[2])
    o_fox = o_fox.reshape(b, s, FOX_WIDTH).astype(x.dtype)

    u = cc * ch
    conv_hist = jnp.zeros((b, CONV_W - 1, CONV_DIM), u.dtype) if prompt else hist[4]
    y_conv, new_conv = _causal_dwconv(u, conv_hist, conv_w)
    o_conv = (cb * y_conv).astype(x.dtype)

    x = x + jnp.concatenate([o_ret, o_fox, o_conv], axis=-1) @ w_out

    h2 = _rms_norm(x, norm_ffn)
    gate_pre = h2 @ w_gate
    ffn_hist = jnp.zeros((b, FFN_CONV_W - 1, D_FF), gate_pre.dtype) if prompt else hist[5]
    gate_c, new_ffn = _causal_dwconv(gate_pre, ffn_hist, ffn_conv_w)
    x = x + (jax.nn.silu(gate_c) * (h2 @ w_up)) @ w_down
    return x, (fkh, fvh, logf, ret_state, new_conv, new_ffn)

def setup_inputs(seed: int = 0) -> dict:
    key = jax.random.key(seed)
    ks = jax.random.split(key, 24)
    f32 = jnp.float32
    nrm = lambda k, shape, sc: jax.random.normal(k, shape, f32) * sc
    return {
        "x_prompt": nrm(ks[0], (BATCH, SEQ, D_MODEL), 1.0),
        "x_sample": nrm(ks[1], (DEC_BATCH, DEC_SEQ, D_MODEL), 1.0),
        "cache_fox_k": nrm(ks[2], (DEPTH, DEC_BATCH, PAST_LEN, FOX_HEADS, FOX_HEAD_DIM), 1.0),
        "cache_fox_v": nrm(ks[3], (DEPTH, DEC_BATCH, PAST_LEN, FOX_HEADS, FOX_HEAD_DIM), 1.0),
        "cache_fox_logf": jax.nn.log_sigmoid(jax.random.uniform(ks[4], (DEPTH, DEC_BATCH, PAST_LEN, FOX_HEADS), f32, 1.0, 6.0)),
        "state_ret": nrm(ks[5], (DEPTH, DEC_BATCH, RET_HEADS, RET_HEAD_DIM, RET_HEAD_DIM), 0.3),
        "state_conv": nrm(ks[6], (DEPTH, DEC_BATCH, CONV_W - 1, CONV_DIM), 1.0),
        "state_ffn_conv": nrm(ks[7], (DEPTH, DEC_BATCH, FFN_CONV_W - 1, D_FF), 1.0),
        "norm_mix": 1.0 + nrm(ks[8], (DEPTH, D_MODEL), 0.02),
        "w_in": nrm(ks[9], (DEPTH, D_MODEL, PROJ_DIM), D_MODEL ** -0.5),
        "ret_gn_gain": 1.0 + nrm(ks[10], (DEPTH, RET_WIDTH), 0.02),
        "fox_q_gain": 1.0 + nrm(ks[11], (DEPTH, FOX_HEADS, FOX_HEAD_DIM), 0.02),
        "fox_k_gain": 1.0 + nrm(ks[12], (DEPTH, FOX_HEADS, FOX_HEAD_DIM), 0.02),
        "fox_f_bias": jax.random.uniform(ks[13], (DEPTH, FOX_HEADS), f32, 1.0, 6.0),
        "conv_w": nrm(ks[14], (DEPTH, CONV_W, CONV_DIM), CONV_W ** -0.5),
        "w_out": nrm(ks[15], (DEPTH, MIX_WIDTH, D_MODEL), MIX_WIDTH ** -0.5),
        "norm_ffn": 1.0 + nrm(ks[16], (DEPTH, D_MODEL), 0.02),
        "w_gate": nrm(ks[17], (DEPTH, D_MODEL, D_FF), D_MODEL ** -0.5),
        "w_up": nrm(ks[18], (DEPTH, D_MODEL, D_FF), D_MODEL ** -0.5),
        "ffn_conv_w": nrm(ks[19], (DEPTH, FFN_CONV_W, D_FF), FFN_CONV_W ** -0.5),
        "w_down": nrm(ks[20], (DEPTH, D_FF, D_MODEL), D_FF ** -0.5),
    }

def reference(x_prompt, x_sample, cache_fox_k, cache_fox_v, cache_fox_logf, state_ret,
              state_conv, state_ffn_conv, norm_mix, w_in, ret_gn_gain, fox_q_gain, fox_k_gain,
              fox_f_bias, conv_w, w_out, norm_ffn, w_gate, w_up, ffn_conv_w, w_down):
    pos_p = jnp.arange(x_prompt.shape[1], dtype=jnp.int32)
    pos_s = PAST_LEN + jnp.arange(x_sample.shape[1], dtype=jnp.int32)
    y_prompt, y_sample = x_prompt, x_sample
    p_st, s_st = [], []
    for l in range(DEPTH):
        prm = (norm_mix[l], w_in[l], ret_gn_gain[l], fox_q_gain[l], fox_k_gain[l], fox_f_bias[l],
               conv_w[l], w_out[l], norm_ffn[l], w_gate[l], w_up[l], ffn_conv_w[l], w_down[l])
        y_prompt, st = _layer(y_prompt, pos_p, None, prm, True)
        p_st.append(st)
        hist = (cache_fox_k[l], cache_fox_v[l], cache_fox_logf[l], state_ret[l],
                state_conv[l], state_ffn_conv[l])
        y_sample, st = _layer(y_sample, pos_s, hist, prm, False)
        s_st.append(st)
    stk = lambda sts, i: jnp.stack([t[i] for t in sts], axis=0)
    return (y_prompt, y_sample,
            stk(p_st, 0), stk(p_st, 1), stk(p_st, 2), stk(p_st, 3), stk(p_st, 4), stk(p_st, 5),
            stk(s_st, 0), stk(s_st, 1), stk(s_st, 2), stk(s_st, 3), stk(s_st, 4), stk(s_st, 5))


_drawn_inputs = setup_inputs


def setup_inputs(seed=0):
    import zlib

    import numpy as np

    out = dict(_drawn_inputs(seed))
    spreads = {}
    factors = {'ret_gn_gain': 6.532, 'fox_q_gain': 8.0, 'fox_k_gain': 2.873}
    for name, (base, spread) in spreads.items():
        noise = np.random.default_rng([zlib.crc32(name.encode()), seed]).standard_normal(out[name].shape)
        drawn = base * np.exp(spread * noise) if base else spread * noise
        out[name] = __import__('jax').numpy.asarray(drawn.astype(out[name].dtype))
    for name, factor in factors.items():
        out[name] = (out[name] * factor).astype(out[name].dtype)
    return out
```

```python
from contextlib import ExitStack

import numpy as np

import concourse.bass as bass
from concourse import mybir

F32 = mybir.dt.float32
F32R = mybir.dt.float32r
BF16 = mybir.dt.bfloat16
ACT = mybir.ActivationFunctionType
ALU = mybir.AluOpType
X = mybir.AxisListType.X

P = 128
D = 1024
KT = D // P
SEQ, NB, NS, PAST = 512, 8, 16, 512
NTOK = SEQ + NB * NS
TT = NTOK // P
TP = SEQ // P
TS = TP
DEPTH = 2
RH, HD, FH = 4, 64, 8
RW, FW, CW = RH * HD, FH * HD, 256
DFF = 2816
PAIRS = DFF // 256
COL_FL = 4 * RW + 3 * FW
COL_CONV = COL_FL + FH
PROJ = COL_CONV + 3 * CW
EPS = 1e-6
HALF = NTOK // 2
PADDED = 2 + SEQ + NB * (NS + 2)
NY = PADDED - 2
NTAP = NB * 2 + 3
NLAST = 2 + NB * 2
NCT = 2 + DFF // P
NEG = -1e30
SLOTS = 3

FL, C0, CC, CH, CB, WO, G0 = 0, 2, 22, 24, 26, 28, 36
SLABS = G0 + 4 + 6 * (PAIRS - 1) + 2
LOOP0 = G0 + 4
DLAST = SLABS - 2
assert SLABS % SLOTS == 0 and 6 % SLOTS == 0

CONST = {}
_at = 0
for _name, _n in (("ident", P), ("cs", TT * 64), ("kdec", TT * RH), ("qdec", 2 * P), ("g16", 2), ("tri", 896),
                  ("tris", P), ("bmask", 16), ("e0", P), ("bsel", NB)):
    CONST[_name] = (_at, _n)
    _at += _n
NCONST = _at


def tables():
    p = np.arange(P)
    gamma = 1.0 - 2.0 ** (-5.0 - np.arange(RH))
    c = np.zeros((P, NCONST), np.float32)

    def put(name, a):
        o, n = CONST[name]
        c[:, o:o + n] = np.asarray(a).reshape(P, n)

    put("ident", np.eye(P))
    pos = np.stack([t * P + p for t in range(TP)] + [PAST + p % NS], 1)
    inv = np.float32(10000.0) ** (-np.arange(HD // 2, dtype=np.float32) / (HD // 2))
    ang = (pos.astype(np.float32)[:, :, None] * inv[None, None, :].astype(np.float32)).astype(np.float64)
    put("cs", np.stack([np.cos(ang), np.sin(ang)], 2))
    left = np.stack([SEQ - 1 - (t * P + p) for t in range(TP)] + [NS - 1 - p % NS], 1)
    put("kdec", gamma[None, None, :] ** left[:, :, None] * HD ** -0.5)
    par = p // HD
    put("qdec", np.stack([gamma[2 * hp + par][:, None] ** (p[None, :] % NS + 1) for hp in range(2)], 1))
    put("g16", np.stack([gamma[2 * hp + par] ** NS for hp in range(2)], 1))
    put("tri", (np.arange(896)[None, :] - 384) >= p[:, None])
    same = (p[:, None] // NS) == (p[None, :] // NS)
    put("tris", same & (p[:, None] <= p[None, :]))
    b8 = np.arange(NB)
    put("bmask", np.tile((p // NS)[:, None] == b8[None, :], (1, 2)))
    put("e0", (p[:, None] % FH) == (p[None, :] // NS))
    put("bsel", ((p % HD) // FH)[:, None] == b8[None, :])
    i = np.arange(SEQ)
    dp = np.where(i[None, None, :] >= p[:, None, None],
                  gamma[None, :, None] ** np.maximum(i[None, None, :] - p[:, None, None], 0), 0.0)
    ds = np.where((same & (p[None, :] >= p[:, None]))[:, None, :],
                  gamma[None, :, None] ** np.maximum(p[None, None, :] - p[:, None, None], 0), 0.0)
    decay = np.concatenate([dp.reshape(P, -1), ds.reshape(P, -1)], 1) * HD ** -0.5
    mb = np.zeros((P, P * (2 + NB)), np.float32)
    mb[:, 0:P] = np.eye(P)
    mb[:, P:2 * P] = np.where(p[None, :] <= p[:, None], 0.0, NEG)
    for b in range(NB):
        seen = (p[None, :] // NS == b) & (p[None, :] % NS <= p[:, None] % NS)
        mb[:, (2 + b) * P:(3 + b) * P] = np.where(seen, 0.0, NEG)
    return c, decay.astype(np.float32), mb


class Banks:

    def __init__(self, full, free):
        self.full, self.free = full, free
        self.n = [0] * 8
        self.jobs = {}
        self.per = None

    def job(self, key, bank):
        assert key not in self.jobs
        self.jobs[key] = (bank, self.n[bank], self.per)
        self.n[bank] += 1

    def loop(self, times, jobs):
        per = [0] * 8
        for _, bank in jobs:
            per[bank] += 1
        self.per = per
        for key, bank in jobs:
            self.job(key, bank)
        for b in range(8):
            self.n[b] += (times - 1) * per[b]
        self.per = None

    def count(self, key, l, it):
        bank, before, per = self.jobs[key]
        v = l * self.n[bank] + (before + 1)
        return v if per is None else v + it * per[bank]

    def bank(self, key):
        return self.jobs[key][0]

    def wait_room(self, eng, key, l, it=None):
        eng.wait_ge(self.free[self.bank(key)], self.count(key, l, it))

    def wait_full_before(self, eng, key, l, it=None):
        eng.wait_ge(self.full[self.bank(key)], self.count(key, l, it) - 1)

    def wait_full(self, eng, key, l, it=None):
        eng.wait_ge(self.full[self.bank(key)], self.count(key, l, it))

    def wait_taken(self, eng, key, l, it=None):
        eng.wait_ge(self.free[self.bank(key)], self.count(key, l, it) + 1)


    def wait_all_taken(self, eng, keys, l):
        last = {self.bank(key): key for key in sorted(keys, key=lambda key: self.jobs[key][1])}
        for key in last.values():
            self.wait_taken(eng, key, l)


def chunk_banks():
    return {0: (3, 4, 5, 6, 7), 1: (3, 4, 5, 6, 7), 2: (5, 6, 7, 1, 2), 3: (1, 2, 0, 3, 4), 4: (7, 1, 2, 0, 3)}


def ret_units():
    return [(h, jb) for h in range(RH) for jb in range(TP)]


def fox_units():
    return [(h, qb) for h in range(FH) for qb in range(TP)]


D_BANKS = (4, 5, 6, 7, 4, 5, 6, 7, 4, 5)
U_BANKS = (6, 7, 4, 5)
STEPS = 3


def batch_jobs(tag, ahead, now):
    jobs = []
    if ahead is not None:
        jobs += [(("kt", tag, p), p % 2) for p in range(4)]
        jobs += [(("ss", tag), 2 + ahead), (("sn", tag), 4 + ahead)]
    if now is not None:
        jobs += [(("pt", tag, 0), 6), (("pt", tag, 1), 7), (("so", tag), 0)]
    return jobs


def down_jobs(tag):
    return [(("d", tag, nc, t), D_BANKS[5 * nc + t]) for nc in range(2) for t in range(TT)]


def plan_banks(banks):
    j = banks.job
    for t in range(TT):
        for g in range(2):
            j(("hT", 0, t, g), (2 * t + g) % 8)
    j("fl", 2)
    cb = chunk_banks()

    def chunk(c):
        for t in range(TT):
            j(("c", c, t), cb[c][t])

    chunk(0)
    j("taps", 2)
    for t in range(TT):
        j(("rt", t), (0, 1, 2, 0, 1)[t])
    chunk(1)
    for n, u in enumerate(ret_units()):
        j(("rs", u), n % 3)
        if n == 0:
            j(("ro", 0), 3)
            j(("ro", 1), 4)
    j("rst", 7)
    j("rss0", 5)
    j("rss1", 6)
    j("rds0", 1)
    j("rds1", 2)
    j("rso", 0)
    j("rsoT", 7)
    chunk(2)
    for t in range(TT):
        j(("qT", t), (3, 4, 0, 3, 4)[t])
    j("cs", 5)
    j("cc", 6)
    j("cn", 7)
    chunk(3)
    for t in range(TT):
        j(("kT", t), (5, 6, 7, 5, 6)[t])
    chunk(4)
    for n, k in enumerate(("cc_", "ch_", "cb_")):
        for i in range(4):
            j((k, i // 2, i % 2), (4 * (n + 1) + i) % 8)
    for n, (h, qb) in enumerate(fox_units()):
        j(("fs", h, qb), n % 3)
        j(("ft", h, qb), 3 + n % 2)
        if h % 2 == 0 and qb == 0:
            j(("fo", h // 2), 5 + (h // 2) % 2)
    for g in range(3):
        j(("orT", g), (7, 0, 1)[g])
    for key, b in batch_jobs("pro", 0, None):
        j(key, b)
    banks.loop(STEPS, batch_jobs("b0", 1, 0) + batch_jobs("b1", 0, 1))
    for key, b in batch_jobs("p6", 1, 0) + batch_jobs("p7", None, 1):
        j(key, b)
    for n in range(2 * TT):
        j(("wo", n // TT, n % TT), n % 8)
    for t in range(TT):
        for g in range(2):
            j(("hT", 1, t, g), (2 + 2 * t + g) % 8)
    for i in range(4):
        j(("g", "pro", i // 2, i % 2), i)
    for i in range(4):
        j(("u", "pro", i // 2, i % 2), U_BANKS[i])
    banks.loop(PAIRS - 1, [(("g", "loop", i // 2, i % 2), i) for i in range(4)] + down_jobs("loop")
               + [(("u", "loop", i // 2, i % 2), U_BANKS[i]) for i in range(4)])
    for key, b in down_jobs("end"):
        j(key, b)
    for g in range(6):
        j(("last", g), (0, 1, 2, 3, 6, 7)[g])


def token_pieces(half):
    return [(0, HALF, 0)] if half == 0 else [(0, SEQ - HALF, HALF), (SEQ - HALF, HALF, None)]


def build(nc, a):
    with ExitStack() as ctx:
        sems = {}

        def sem(name):
            sems[name] = ctx.enter_context(nc.semaphore(name))
            return sems[name]

        bank = [ctx.enter_context(nc.psum_tensor(f"bank{i}", [P, 512], F32)) for i in range(8)]
        B = Banks([sem(f"full{i}") for i in range(8)], [sem(f"free{i}") for i in range(8)])
        plan_banks(B)

        base = (nc.sbuf_base + 31) // 32 * 32
        size = {F32: 4, F32R: 4, BF16: 2}
        top = [base]

        def at(name, shape, dt, offset):
            n = size[dt]
            for s in shape[1:]:
                n *= s
            return nc.alloc_sbuf_tensor_at(name, shape, dt, offset=offset), offset + (n + 31) // 32 * 32

        def own(name, shape, dt=F32):
            t, top[0] = at(name, shape, dt, top[0])
            return t

        def region(*groups):
            start, ends, out = top[0], [], []
            for g in groups:
                o = start
                for name, shape, dt in g:
                    t, o = at(name, shape, dt, o)
                    out.append(t)
                ends.append(o)
            top[0] = max(ends)
            return out

        const = own("const", [P, NCONST])

        def K(name):
            o, n = CONST[name]
            return const[:, o:o + n]

        maskb = own("maskb", [P, (2 + NB) * P], BF16)
        raw = own("raw", [P, SLOTS, 1024])
        whi = own("whi", [P, SLOTS, 1024], F32R)
        wlo = own("wlo", [P, SLOTS, 1024], F32R)
        x = own("x", [P, TT, D])
        hhi = own("hhi", [P, KT, NTOK], F32R)
        hlo = own("hlo", [P, KT, NTOK], F32R)
        taps = own("taps", [P, NCT, NTAP])
        last = own("last", [P, NCT, NLAST])
        sel = own("sel", [P, FH, P], F32R)
        ncp = own("ncp", [P, SEQ], F32R)
        ncn = own("ncn", [P, P], F32R)
        lf = own("lf", [P, TT, FH])
        lfx = own("lfx", [P, TP, 40])
        small = own("small", [P, 544])
        mhalf = own("mhalf", [P, 40])
        pst = own("pst", [P, 2, HD])
        ctot = own("ctot", [P, 1])
        wcn = own("wcn", [P, P])
        wcnh = own("wcnh", [P, P], F32R)
        fbias = own("fbias", [P, FH])
        ftap = own("ftap", [P, 2, 3])
        (fqg, fkg, gng, qbd) = region(
            [("fqg", [P, FW], F32), ("fkg", [P, FW], F32), ("gng", [P, RW], F32)],
            [("qbd", [P, 2, 640], F32)])
        (gains, os_, ncc) = region(
            [("gains", [P, D], F32)],
            [("os", [P, 4, P], F32), ("ncc", [P, PAST], F32R)])
        eb = own("eb", [P, 2, P], F32R)
        (fqT, fkT, fv, guhi, gulo, gact) = region(
            [("fqT", [P, 4, NTOK], F32), ("fkT", [P, 4, NTOK], F32), ("fv", [P, TT, FW], F32)],
            [("guhi", [P, 2, NTOK], F32R), ("gulo", [P, 2, NTOK], F32R), ("gact", [P, 2, NY], F32)])
        gs = own("gs", [P, TT, RW])
        (rT, kw, rv, decp, decs, s0, kb, kT, vb, rows, gpad, gu, _, lrows) = region(
            [("rT", [P, 4, NTOK], F32), ("kw", [P, TT, RW], F32), ("rv", [P, TT, RW], F32),
             ("decp", [P, RH, SEQ], F32), ("decs", [P, RH, P], F32), ("s0", [P, 2, NB * HD], F32)],
            [("kb", [P, 4, FW], F32), ("kT", [P, 4, PAST], F32), ("vb", [P, 2, 4, FW], F32)],
            [("rows", [NTAP, CW + DFF], F32)],
            [("gpad", [P, 2, PADDED], F32), ("gu", [P, 2, NTOK], F32), ("gap", [P, 512], F32),
             ("lrows", [NLAST, CW + DFF], F32)])
        (upad, ccs, gnd, gnsq, lc, lcd, lexp, nct) = region(
            [("upad", [P, 2, PADDED], F32), ("ccs", [P, 2, NTOK], F32)],
            [("gnd", [P, TT * RH, HD], F32), ("gnsq", [P, TT * RH, HD], F32)],
            [("lc", [P, 4, 64], F32), ("lcd", [P, 4, 2, 64], F32), ("lexp", [P, P], F32),
             ("nct", [P, 512], F32R)])
        (xn, tA, n2, n1, ptr, vm, rso, qw, oc, ycv, pf, pTf, ps, pTs) = region(
            [("xn", [P, 2, D], F32)],
            [("tA", [P, 2, 512], F32), ("n2", [P, 2, 512], F32), ("n1", [P, 512], F32)],
            [("ptr", [P, 3, 512], F32), ("vm", [P, 2, 512], F32), ("rso", [P, 2 * P], F32),
             ("qw", [P, 2, P], F32)],
            [("oc", [P, 2, NTOK], F32), ("ycv", [P, 2, NY], F32)],
            [("pf", [P, 3, 512], F32), ("pTf", [P, 2, 512], F32)],
            [("ps", [P, 2, 640], F32), ("pTs", [P, 2, 640], F32)])

        SS, VAR, RS = 0, 8, 16
        FSS, FVAR, FRS = (32, 176), (80, 224), (128, 272)
        GS, GM, GQ, GV, GR = 320, 340, 360, 380, 400
        NM, RSUM, REC = 420, 452, 484
        SB = 516

        def col(c, n=1, rows_=P):
            return small[0:rows_, c:c + n]

        consts_in = sem("consts_in")
        x_in = sem("x_in")
        pool_const = sem("pool_const")
        sel_ready = sem("sel_ready")
        raw_in = [sem(f"raw_in{i}") for i in range(SLOTS)]
        hi_split = sem("hi_split")
        lo_split = sem("lo_split")
        slab_used = sem("slab_used")
        rows_in = sem("rows_in")
        gains_in = sem("gains_in")
        foxg_in = sem("foxg_in")
        lc_in = sem("lc_in")
        dec_in = sem("dec_in")
        s0_in = sem("s0_in")
        k_in = sem("k_in")
        v_in = [sem(f"v_in{i}") for i in range(2)]
        x_done = sem("x_done")
        sumsq = sem("sumsq")
        rstd = sem("rstd")
        xn_ready = sem("xn_ready")
        h_hi = sem("h_hi")
        fl_z = sem("fl_z")
        fl_e = sem("fl_e")
        lf_ready = sem("lf_ready")
        lcd_ready = sem("lcd_ready")
        nct_ready = sem("nct_ready")
        nc_ready = sem("nc_ready")
        wcn_ready = sem("wcn_ready")
        lexp_ready = sem("lexp_ready")
        vm_used = sem("vm_used")
        rot_ready = sem("rot_ready")
        kw_ready = sem("kw_ready")
        silu_ready = sem("silu_ready")
        gs_ready = sem("gs_ready")
        qw_ready = sem("qw_ready")
        vm_ready = sem("vm_ready")
        s_new = sem("s_new")
        gn_d = sem("gn_d")
        gn_sq = sem("gn_sq")
        gn_v = sem("gn_v")
        gn_r = sem("gn_r")
        oret = sem("oret")
        fsq = sem("fsq")
        fss = sem("fss")
        frs = sem("frs")
        fn_ready = sem("fn_ready")
        k_stored = [sem(f"k_stored{i}") for i in range(2)]
        stores = sem("stores")
        hist_u = sem("hist_u")
        u_ready = sem("u_ready")
        cat_hi = sem("cat_hi")
        cat_lo = sem("cat_lo")
        nmax = sem("nmax")
        pnorm = sem("pnorm")
        q_ready = sem("q_ready")
        smax = sem("smax")
        snorm = sem("snorm")
        gpad_hist = sem("gpad_hist")
        gconv = sem("gconv")
        gsilu = sem("gsilu")
        gu_hi = sem("gu_hi")
        gu_ready = sem("gu_ready")
        glast = sem("glast")

        used_index = {}
        final = {}

        def mark(first, n, key):
            for s_ in range(first, first + n - 1):
                used_index[s_] = len(used_index)
            final[first + n - 1] = key

        mark(FL, 2, "fl")
        for c in range(5):
            mark(C0 + 4 * c, 4, ("c", c, 4))
        for first, k in ((CC, "cc_"), (CH, "ch_"), (CB, "cb_")):
            mark(first, 2, (k, 1, 1))
        for n in range(2):
            mark(WO + 4 * n, 4, ("wo", n, 4))
        mark(G0, 2, ("g", "pro", 1, 1))
        mark(G0 + 2, 2, ("u", "pro", 1, 1))
        USED0 = len(used_index)
        USED = USED0 + 2 * (PAIRS - 1)
        STORES = 14
        HIS, CATS = 9, 2

        def wait_used(eng, n, l, it=None):
            if it is not None:
                j = n
                if j < 0:
                    assert j == -1
                    eng.wait_ge(B.full[B.bank(("d", "loop", 0, 1))], B.count(("d", "loop", 0, 1), l, it) - 1)
                elif j in (0, 4):
                    eng.wait_ge(slab_used, l * USED + it * 2 + (USED0 + 1 + j // 4))
                else:
                    key = {1: ("g", "loop", 1, 1), 2: ("d", "loop", 0, 4), 3: ("d", "loop", 1, 4)}[j]
                    B.wait_full(eng, key, l, it)
            elif n >= 0:
                if n in used_index:
                    eng.wait_ge(slab_used, l * USED + used_index[n] + 1)
                else:
                    B.wait_full(eng, final[n], l)

        def wait_k_stored(eng, t, l):
            half = t % 2
            eng.wait_ge(k_stored[half], l * (16 * ((TT + 1 - half) // 2)) + 16 * (t // 2 + 1))

        def slot(n):
            return n % SLOTS

        LPS = SLABS // SLOTS

        def wait_loaded(eng, n, l, it=None):
            v = l * (16 * LPS) + 16 * (n // SLOTS + 1)
            eng.wait_ge(raw_in[slot(n)], v if it is None else v + it * 32)

        def nth(n, l, it=None, more=1):
            v = l * SLABS + n + more
            return v if it is None else v + it * 6

        def width(n):
            return 32 if n < C0 else 1024

        parted = sem("parted")

        def apart(eng):
            eng.sem_inc(parted, 1)

        block = ctx.enter_context(nc.Block())

        @block.sync
        def _(sp):
            sp.dma_start(const[:, :], a["c_tables"]).then_inc(consts_in, 16)
            for t in range(TP):
                sp.dma_start(x[:, t, :], a["x_prompt"][0, t * P:(t + 1) * P, :]).then_inc(x_in, 16)
            sp.dma_start(x[:, TS, :], a["x_sample"].rearrange("b s d -> (b s) d")).then_inc(x_in, 16)
            sp.dma_start(maskb[:, :], a["c_masks"]).then_inc(consts_in, 16)

            def w_tile(w, l, k, nk, c, n):
                return w[bass.ds(l, 1)].rearrange("o (k p) n -> p (o k) n", p=P)[:, k:k + nk, c:c + n]

            def load(n, l, src, it=None):
                sp.wait_ge(lo_split, nth(n, l, it, 1))
                apart(sp)
                dst = raw[:, slot(n), 0:width(n)].rearrange("p (k n) -> p k n", k=src.shape[1])
                sp.dma_start(dst, src).then_inc(raw_in[slot(n)], 16)

            def slab_src(n, l):
                w = a["w_in"]
                if n < C0:
                    return w_tile(w, l, 4 * n, 4, COL_FL, FH)
                if n < CC:
                    c, i = divmod(n - C0, 4)
                    return w_tile(w, l, 2 * i, 2, 512 * c, 512)
                if n < WO:
                    c, i = divmod(n - CC, 2)
                    return w_tile(w, l, 4 * i, 4, COL_CONV + CW * (1, 2, 0)[c], CW)
                if n < G0:
                    c, i = divmod(n - WO, 4)
                    return w_tile(a["w_out"], l, 2 * i, 2, 512 * c, 512)
                w, i = (a["w_gate"], n - G0) if n < G0 + 2 else (a["w_up"], n - G0 - 2)
                return w_tile(w, l, 4 * i, 4, 0, 256)

            def up_src(w, l, it, i):
                v = w[bass.ds(l, 1)].rearrange("o (k p) n -> p (o k) n", p=P)
                return v[:, 4 * i:4 * i + 4, bass.ds(it * 256 + 256, 256)]

            def down_src(l, it, c):
                v = a["w_down"][bass.ds(l, 1), bass.ds(it * 256, 256) if it is not None else
                                slice((PAIRS - 1) * 256, DFF), :]
                return v.rearrange("o (k p) n -> p (o k) n", p=P)[:, :, 512 * c:512 * c + 512]

            kview = a["cache_fox_k"].rearrange("l b (k p) h d -> (l b) p k (h d)", p=P)
            vview = a["cache_fox_v"].rearrange("l b (k p) h d -> (l b) p k (h d)", p=P)

            def load_k(l, b):
                sp.dma_start(kb[:, :, :], kview[bass.ds(l * NB + b, 1)].rearrange("o p k n -> p (o k) n"))\
                    .then_inc(k_in, 16)

            def load_v(l, b, u):
                sp.dma_start(vb[:, u], vview[bass.ds(l * NB + b, 1)].rearrange("o p k n -> p (o k) n"))\
                    .then_inc(v_in[u], 16)

            with sp.Fori(0, DEPTH) as l:
                def one(name):
                    return a[name][bass.ds(l, 1)]

                for n in range(3):
                    load(n, l, slab_src(n, l))
                sp.dma_start(gains[:, :], one("norm_mix").to_broadcast([P, D])).then_inc(gains_in, 16)
                sp.dma_start(fbias[:, :], one("fox_f_bias").to_broadcast([P, FH])).then_inc(foxg_in, 16)
                sp.dma_start(rows[0:16, 0:CW], one("state_conv").rearrange("o b w c -> (o b w) c")).then_inc(rows_in, 16)
                sp.dma_start(rows[0:16, CW:], one("state_ffn_conv").rearrange("o b w c -> (o b w) c")).then_inc(rows_in, 16)
                sp.dma_start(rows[16:19, 0:CW], one("conv_w").rearrange("o w c -> (o w) c")).then_inc(rows_in, 16)
                sp.dma_start(rows[16:19, CW:], one("ffn_conv_w").rearrange("o w c -> (o w) c")).then_inc(rows_in, 16)
                sp.dma_start(fqg[:, :], one("fox_q_gain").rearrange("o h d -> o (h d)").to_broadcast([P, FW])).then_inc(foxg_in, 16)
                sp.dma_start(fkg[:, :], one("fox_k_gain").rearrange("o h d -> o (h d)").to_broadcast([P, FW])).then_inc(foxg_in, 16)
                sp.dma_start(gng[:, :], one("ret_gn_gain").to_broadcast([P, RW])).then_inc(foxg_in, 16)
                sp.dma_start(decp[:, :, :], a["c_decay"][:, 0:RH * SEQ]).then_inc(dec_in, 16)
                sp.dma_start(decs[:, :, :], a["c_decay"][:, RH * SEQ:]).then_inc(dec_in, 16)
                for hp in range(2):
                    for par in range(2):
                        sp.dma_start(s0[64 * par:64 * par + 64, hp, :].rearrange("d (b e) -> d b e", b=NB),
                                     one("state_ret").rearrange("o b h d e -> h d (o b) e")[2 * hp + par])\
                            .then_inc(s0_in, 16)
                for n in range(3, 10):
                    load(n, l, slab_src(n, l))
                sp.wait_ge(lf_ready, l + 1)
                sp.dma_start(a["p_fox_logf"][bass.ds(l, 1)].rearrange("o b (t p) h -> p (o b t) h", p=P),
                             lf[:, 0:TP, :]).then_inc(stores, 16)
                sp.dma_start(a["s_fox_logf"][bass.ds(l, 1)].rearrange("o b s h -> (o b s) h"),
                             lf[:, TS, :]).then_inc(stores, 16)
                for n in range(10, 14):
                    load(n, l, slab_src(n, l))
                B.wait_taken(sp, "rst", l)
                for hp in range(2):
                    sp.dma_start(a["p_ret"][bass.ds(l, 1)].rearrange("o b h d e -> (o b h d) e")
                                 [P * hp:P * hp + P, :], pst[:, hp, :]).then_inc(stores, 16)
                sp.wait_ge(s_new, l + 1)
                for hp in range(2):
                    for par in range(2):
                        sp.dma_start(a["s_ret"][bass.ds(l, 1)].rearrange("o b h d e -> h d (o b) e")[2 * hp + par],
                                     s0[64 * par:64 * par + 64, hp, :].rearrange("d (b e) -> d b e", b=NB))\
                            .then_inc(stores, 16)
                for n in range(14, 18):
                    load(n, l, slab_src(n, l))
                sp.wait_ge(oret, l + 1)
                for blk in range(4):
                    sp.dma_start(lc[:, blk, :].rearrange("p (b h) -> p b h", b=NB),
                                 one("cache_fox_logf").rearrange("o b (k p) h -> k p (o b) h", p=P)[blk])\
                        .then_inc(lc_in, 16)
                for n in range(18, 23):
                    load(n, l, slab_src(n, l))
                for t in range(TT):
                    sp.wait_ge(fn_ready, l * (2 * TT) + TT + t + 1)
                    if t < TP:
                        dst = a["p_fox_k"][bass.ds(l, 1)].rearrange("o b s h d -> (o b s) (h d)")[t * P:(t + 1) * P, :]
                    else:
                        dst = a["s_fox_k"][bass.ds(l, 1)].rearrange("o b s h d -> (o b s) (h d)")
                    sp.dma_start(dst, n2[:, t % 2, :]).then_inc(k_stored[t % 2], 16)
                for n in range(23, 27):
                    load(n, l, slab_src(n, l))
                B.wait_taken(sp, ("c", 4, TT - 1), l)
                sp.dma_start(a["p_fox_v"][bass.ds(l, 1)].rearrange("o b (t p) h d -> p (o b t) (h d)", p=P),
                             fv[:, 0:TP, :]).then_inc(stores, 16)
                sp.dma_start(a["s_fox_v"][bass.ds(l, 1)].rearrange("o b s h d -> (o b s) (h d)"),
                             fv[:, TS, :]).then_inc(stores, 16)
                for n in range(27, 31):
                    load(n, l, slab_src(n, l))
                B.wait_full(sp, "rsoT", l)
                sp.wait_ge(stores, l * (16 * STORES) + 16 * 10)
                load_k(l, 0)
                load_v(l, 0, 0)
                load_v(l, 1, 1)
                B.wait_full(sp, ("kt", "pro", 3), l)
                load_k(l, 1)
                with sp.Fori(0, STEPS) as it:
                    for u in range(2):
                        B.wait_full(sp, ("kt", f"b{u}", 3), l, it)
                        load_k(l, it * 2 + (u + 2))
                        B.wait_full(sp, ("so", f"b{u}"), l, it)
                        load_v(l, it * 2 + (u + 2), u)
                sp.wait_ge(cat_lo, l * CATS + CATS)
                sp.dma_start(gains[:, :], one("norm_ffn").to_broadcast([P, D])).then_inc(gains_in, 16)
                for n in range(31, LOOP0):
                    load(n, l, slab_src(n, l))
                with sp.Fori(0, PAIRS - 1) as it:
                    for j in range(6):
                        src = (up_src(a["w_gate"], l, it, j) if j < 2 else down_src(l, it, j - 2) if j < 4
                               else up_src(a["w_up"], l, it, j - 4))
                        load(LOOP0 + j, l, src, it)
                for c in range(2):
                    load(DLAST + c, l, down_src(l, None, c))
                for g in range(6):
                    B.wait_taken(sp, ("last", g), l)
                    apart(sp)
                for k_, (p_, s_), c0, c1 in ((0, ("p_conv", "s_conv"), 0, CW), (1, ("p_ffn", "s_ffn"), CW, CW + DFF)):
                    sp.dma_start(a[p_][bass.ds(l, 1)].rearrange("o b w c -> (o b w) c"), lrows[0:2, c0:c1]).then_inc(stores, 16)
                    sp.dma_start(a[s_][bass.ds(l, 1)].rearrange("o b w c -> (o b w) c"), lrows[2:18, c0:c1]).then_inc(stores, 16)
                sp.wait_ge(stores, l * (16 * STORES) + 16 * STORES)
                wait_k_stored(sp, TT - 2, l)
                wait_k_stored(sp, TT - 1, l)
                apart(sp)

            sp.wait_ge(x_done, 2 * TT * (DEPTH + 1))
            for t in range(TP):
                sp.dma_start(a["y_prompt"][0, t * P:(t + 1) * P, :], x[:, t, :]).then_inc(x_in, 16)
            sp.dma_start(a["y_sample"].rearrange("b s d -> (b s) d"), x[:, TS, :]).then_inc(x_in, 16)
            sp.wait_ge(x_in, 16 * 2 * TT)

        @block.gpsimd
        def _(pool):
            for b in range(8):
                pool.sem_inc(B.free[b], 1)
            pool.sem_inc(lo_split, SLOTS)
            pool.sem_inc(x_done, 2 * TT)
            pool.memset(mhalf[:, :], -0.5)
            pool.memset(lfx[:, :, :], 0.0)
            pool.memset(ncp[:, :].bitcast(F32), 0.0)
            pool.memset(small[:, :], 0.0)
            pool.drain().then_inc(pool_const, 1)
            pool.wait_ge(consts_in, 32)

            def rsqrt(ss, var, rs, n, scale, done):
                pool.tensor_scalar(col(var, n), col(ss, n), scale, EPS, ALU.mult, ALU.add)
                pool.drain()
                pool.tensor_tensor(col(rs, n), col(var, n), mhalf[:, 0:n], ALU.pow).then_inc(done, 1)

            def norm(which, l):
                for t in range(TT):
                    pool.wait_ge(sumsq, l * (2 * TT) + which * TT + t + 1)
                    apart(pool)
                    rsqrt(SS + t, VAR + t, RS + t, 1, 1.0 / D, rstd)

            def pads(u, ft, hist, n):
                dst = u[:, ft:ft + n, 2 + SEQ:].rearrange("p f (b s) -> p f b s", b=NB)[:, :, :, 0:2]
                for f in range(n):
                    src = hist[f]
                    yield dst[:, f], src

            with pool.Fori(0, DEPTH) as l:
                norm(0, l)
                pool.wait_ge(foxg_in, l * 64 + 64)
                apart(pool)
                pool.tensor_scalar(fqg[:, :], fqg[:, :], HD ** -0.5, None, ALU.mult)
                for t in range(TT):
                    pool.wait_ge(rot_ready, l * TT + t + 1)
                    B.wait_full(pool, "taps", l) if t == 0 else None
                    pool.tensor_tensor(kw[:, t, :].rearrange("p (h d) -> p h d", h=RH),
                                       n2[:, t % 2, 256:512].rearrange("p (h d) -> p h d", h=RH),
                                       K("kdec").rearrange("p (t h) -> p t h", t=TT)[:, t, :].unsqueeze(2).to_broadcast([P, RH, HD]),
                                       ALU.mult).then_inc(kw_ready, 1)
                for t in range(TT):
                    pool.wait_ge(silu_ready, l * TT + t + 1)
                    pool.tensor_tensor(gs[:, t, :], gs[:, t, :], gng[:, :], ALU.mult)
                pool.drain().then_inc(gs_ready, 1)
                pool.wait_ge(gn_v, l + 1)
                apart(pool)
                rsqrt(GV, GQ, GR, TT * RH, 1.0 / HD, gn_r)
                for t in range(TT):
                    pool.wait_ge(fss, l * (2 * TT) + t + 1)
                    apart(pool)
                    rsqrt(FSS[0] + 8 * t, FVAR[0] + 8 * t, FRS[0] + 8 * t, FH, 1.0 / HD, frs)
                pool.wait_ge(lc_in, l * 64 + 64)
                apart(pool)
                pool.tensor_copy(lcd[:, :, 0, :], lc[:, :, :])
                pool.tensor_copy(lcd[:, :, 1, :], lc[:, :, :])
                pool.drain().then_inc(lcd_ready, 1)
                for t in range(TT):
                    pool.wait_ge(fss, l * (2 * TT) + TT + t + 1)
                    apart(pool)
                    rsqrt(FSS[1] + 8 * t, FVAR[1] + 8 * t, FRS[1] + 8 * t, FH, 1.0 / HD, frs)
                pool.wait_ge(nc_ready, l + 1)
                B.wait_taken(pool, "taps", l)
                apart(pool)
                pool.memset(upad[:, :, 0:2], 0.0)
                for ft in range(2):
                    pool.tensor_copy(upad[:, ft, 2 + SEQ:].rearrange("p (b s) -> p b s", b=NB)[:, :, 0:2],
                                     taps[:, ft, 0:16].rearrange("p (b w) -> p b w", b=NB))
                pool.drain().then_inc(hist_u, 1)
                pool.wait_ge(u_ready, l + 1)
                apart(pool)
                for ft in range(2):
                    pool.tensor_copy(last[:, ft, 0:2], upad[:, ft, SEQ:SEQ + 2])
                    pool.tensor_copy(last[:, ft, 2:18].rearrange("p (b w) -> p b w", b=NB),
                                     upad[:, ft, 2 + SEQ:].rearrange("p (b s) -> p b s", b=NB)[:, :, NS:NS + 2])

                def queries(b, u):
                    for par in range(2):
                        dst = qbd[64 * par:64 * par + 64, u, :].rearrange("p (c s) -> p c s", c=4)[:, :, 16 * par:16 * par + 16]
                        src = fqT[64 * par:64 * par + 64, :, SEQ:][:, :, bass.ds(b * 16, 16)]
                        pool.tensor_copy(dst, src)
                        pool.drain()
                    pool.tensor_tensor(eb[:, u, :], K("e0"), K("bsel")[:, bass.ds(b, 1)].to_broadcast([P, P]), ALU.mult)
                    pool.drain().then_inc(q_ready, 1)

                pool.wait_ge(fn_ready, l * (2 * TT) + 2 * TT)
                B.wait_taken(pool, ("qT", TT - 1), l)
                apart(pool)
                pool.memset(qbd[:, :, :], 0.0)
                pool.drain()
                B.wait_taken(pool, ("fs", FH - 1, TP - 1), l)
                apart(pool)
                queries(0, 0)
                with pool.Fori(0, STEPS) as it:
                    for u in range(2):
                        B.wait_full_before(pool, ("sn", f"b{u}"), l, it)
                        apart(pool)
                        queries(it * 2 + (u + 1), 1 - u)
                B.wait_full(pool, ("sn", "b0"), l, STEPS - 1)
                apart(pool)
                queries(NB - 1, 1)

                norm(1, l)
                pool.wait_ge(cat_lo, l * CATS + CATS)
                apart(pool)
                pool.memset(gpad[:, :, 0:2], 0.0)

                def ffn_pads(c):
                    for f in range(2):
                        tp = taps[:, bass.ds(c + f, 1), :] if not isinstance(c, int) else taps[:, c + f:c + f + 1, :]
                        pool.tensor_copy(gpad[:, f, 2 + SEQ:].rearrange("p (b s) -> p b s", b=NB)[:, :, 0:2],
                                         tp[:, 0, 0:16].rearrange("p (b w) -> p b w", b=NB))
                        pool.tensor_copy(ftap[:, f:f + 1, :], tp[:, :, 16:19])
                    pool.drain().then_inc(gpad_hist, 1)

                def ffn_last(c):
                    for f in range(2):
                        lp = last[:, bass.ds(c + f, 1), :] if not isinstance(c, int) else last[:, c + f:c + f + 1, :]
                        pool.tensor_copy(lp[:, 0, 0:2], gpad[:, f, SEQ:SEQ + 2])
                        pool.tensor_copy(lp[:, 0, 2:18].rearrange("p (b w) -> p b w", b=NB),
                                         gpad[:, f, 2 + SEQ:].rearrange("p (b s) -> p b s", b=NB)[:, :, NS:NS + 2])
                    pool.drain().then_inc(glast, 1)

                ffn_pads(2)
                pool.wait_ge(gconv, l * (2 * PAIRS) + 2)
                apart(pool)
                ffn_last(2)
                with pool.Fori(0, PAIRS - 1) as it:
                    ffn_pads(it * 2 + 4)
                    pool.wait_ge(gconv, l * (2 * PAIRS) + it * 2 + 4)
                    apart(pool)
                    ffn_last(it * 2 + 4)

        @block.scalar
        def _(act):
            split_to = [0]

            def split(n, l, it=None):
                wait_loaded(act, n, l, it)
                act.activation(whi[:, slot(n), 0:width(n)], raw[:, slot(n), 0:width(n)], ACT.Copy).then_inc(hi_split, 1)

            def upto(n, l):
                while split_to[0] <= n:
                    wait_used(act, split_to[0] - SLOTS, l)
                    split(split_to[0], l)
                    split_to[0] += 1

            def split_loop(j, l, it):
                wait_used(act, j - SLOTS, l, it)
                split(LOOP0 + j, l, it)

            def norm(which, l, splits):
                for t in range(TT + 1):
                    if t < TT:
                        act.wait_ge(x_done, l * (2 * TT) + (which * TT + TT + t + 1))
                        if t >= 2:
                            B.wait_full(act, ("hT", which, t - 2, 1), l)
                        act.activation(xn[:, t % 2, :], x[:, t, :], ACT.Square, accum_out=col(SS + t)).then_inc(sumsq, 1)
                    if t > 0:
                        for g in range(2):
                            B.wait_full(act, ("hT", which, t - 1, g), l)
                            act.activation(hhi[:, 4 * g:4 * g + 4, (t - 1) * P:t * P],
                                           bank[B.bank(("hT", which, t - 1, g))][:, :].rearrange("p (k n) -> p k n", k=4),
                                           ACT.Copy).then_inc(h_hi, 1)
                    if t in splits:
                        upto(splits[t], l)

            act.wait_ge(x_in, 16 * TT)
            act.wait_ge(pool_const, 1)
            with act.Fori(0, DEPTH) as l:
                split_to[0] = 0

                def evac(key, out, l, it=None, view=None):
                    B.wait_full(act, key, l, it)
                    src = bank[B.bank(key)][:, :] if view is None else view(bank[B.bank(key)])
                    act.activation(out, src, ACT.Copy).then_inc(B.free[B.bank(key)], 1)

                def quad(b):
                    return b[:, :].rearrange("p (c n) -> p c n", c=4)

                norm(0, l, {0: 0, 1: 1, 2: 2})
                upto(3, l)
                act.wait_ge(fl_z, l * 2 + 1)
                act.activation(n1[:, 80:120], n1[:, 40:80], ACT.Exp, scale=-1.0).then_inc(fl_e, 1)
                act.wait_ge(fl_z, l * 2 + 2)
                act.activation(n1[:, 160:200], n1[:, 120:160], ACT.Ln).then_inc(fl_e, 1)
                upto(C0 + 6, l)
                evac("taps", taps[:, :, :], l, view=lambda b: b[:, 0:NCT * NTAP].rearrange("p (c n) -> p c n", c=NCT))
                for t in range(TT):
                    evac(("rt", t), rT[:, :, t * P:(t + 1) * P], l, view=quad)
                upto(C0 + 9, l)
                for t in range(TT):
                    B.wait_full(act, ("c", 1, t), l)
                    bk = bank[B.bank(("c", 1, t))]
                    act.activation(gs[:, t, :], bk[:, 256:512], ACT.Silu).then_inc(silu_ready, 1)
                    act.activation(rv[:, t, :], bk[:, 0:256], ACT.Copy).then_inc(B.free[B.bank(("c", 1, t))], 1)
                upto(C0 + 10, l)
                evac("rst", pst[:, :, :], l, view=lambda b: b[:, 0:2 * HD].rearrange("p (c n) -> p c n", c=2))
                evac("rso", rso[:, :], l, view=lambda b: b[:, 0:2 * P])
                act.wait_ge(gn_d, l + 1)
                act.activation(gnsq[:, :, :], gnd[:, :, :], ACT.Square).then_inc(gn_sq, 1)
                for c in (2, 3):
                    k_ = C0 + 4 * c + 3
                    upto(k_ + 2, l)
                    for t in range(TT):
                        B.wait_full(act, ("c", c, t), l)
                        n_ = (c - 2) * TT + t
                        if n_ >= 2:
                            act.wait_ge(fss, l * (2 * TT) + (n_ - 1))
                        act.activation(tA[:, t % 2, :], bank[B.bank(("c", c, t))][:, :], ACT.Square).then_inc(fsq, 1)
                        if t == 1:
                            upto(k_ + 3, l)
                    if c == 2:
                        for t in range(TT):
                            evac(("qT", t), fqT[:, :, t * P:(t + 1) * P], l, view=quad)
                        act.wait_ge(oret, l + 1)
                        for key, dst, r_, r0 in (("cs", ncp, 8, 32), ("cc", ncc, 64, 64)):
                            B.wait_full(act, key, l)
                            bk = bank[B.bank(key)]
                            act.activation(dst[0:r_, :], bk[0:r_, :], ACT.Copy, scale=-1.0)
                            act.activation(nct[r0:r0 + r_, :], bk[r0:r0 + r_, :], ACT.Copy, scale=-1.0).then_inc(nct_ready, 1)
                        act.wait_ge(wcn_ready, l + 1)
                        act.activation(ncn[0:64, :], wcn[0:64, :], ACT.Copy)
                        act.activation(wcnh[64:128, :], wcn[64:128, :], ACT.Copy).then_inc(nct_ready, 1)
                        upto(k_ + 4, l)
                    else:
                        for t in range(TT):
                            evac(("kT", t), fkT[:, :, t * P:(t + 1) * P], l, view=quad)
                        upto(k_ + 4, l)
                k_ = C0 + 19
                upto(k_ + 2, l)
                for t in range(TT):
                    evac(("c", 4, t), fv[:, t, :], l)
                    if t == 1:
                        upto(k_ + 3, l)
                upto(k_ + 4, l)
                act.wait_ge(nc_ready, l + 1)
                for i in range(4):
                    ft, half = i // 2, i % 2
                    evac(("cc_", ft, half), ccs[:, ft, half * HALF:(half + 1) * HALF], l, view=lambda b: b[:, 0:HALF])
                upto(WO + 2, l)
                B.wait_taken(act, ("cb_", 1, 1), l)
                act.activation(hhi[:, 6:8, :], oc[:, :, :], ACT.Copy).then_inc(cat_hi, 1)
                units = fox_units()
                NU = len(units)
                for n in range(NU + 3):
                    if n < NU:
                        h, qb = units[n]
                        N = P * (qb + 1)
                        key = ("fs", h, qb)
                        act.wait_ge(nmax, l * NU + n + 1)
                        act.activation(pf[:, n % 3, 0:N], bank[B.bank(key)][:, 0:N], ACT.Exp, bias=col(NM + n),
                                       accum_out=col(RSUM + n)).then_inc(B.free[B.bank(key)], 1)
                    if 2 <= n < NU + 2:
                        h, qb = units[n - 2]
                        N = P * (qb + 1)
                        evac(("ft", h, qb), pTf[:, n % 2, 0:N], l, view=lambda b: b[:, 0:N])
                    if n >= 3:
                        h, qb = units[n - 3]
                        if h % 2 and qb == TP - 1:
                            key = ("fo", h // 2)
                            B.wait_full(act, key, l)
                            act.activation(hhi[:, 2 + h // 2, 0:SEQ], bank[B.bank(key)][:, :], ACT.Copy).then_inc(cat_hi, 1)
                for g in range(3):
                    w_ = 256 if g < 2 else P
                    B.wait_full(act, ("orT", g), l)
                    act.activation(hhi[:, 0:2, 256 * g:256 * g + w_],
                                   bank[B.bank(("orT", g))][:, :].rearrange("p (r c) -> p r c", r=2)[:, :, 0:w_],
                                   ACT.Copy).then_inc(cat_hi, 1)

                def step(tag, ahead, now, nb, it=None):
                    if ahead is not None:
                        for p_ in (0, 2):
                            evac(("kt", tag, p_), kT[:, p_, :], l, it)
                        act.wait_ge(smax, nb)
                        o = SB + 8 * ahead
                        for key, c0, n_, acc in ((("ss", tag), 0, 512, 3), (("sn", tag), 512, P, 4)):
                            act.activation(ps[:, ahead, c0:c0 + n_], bank[B.bank(key)][:, 0:n_], ACT.Exp, bias=col(o + 2),
                                           accum_out=col(o + acc)).then_inc(B.free[B.bank(key)], 1)
                    if now is not None:
                        evac(("pt", tag, 0), pTs[:, now, 0:512], l, it)

                step("pro", 0, None, l * NB + 1)
                with act.Fori(0, STEPS) as it:
                    step("b0", 1, 0, l * NB + it * 2 + 2, it)
                    step("b1", 0, 1, l * NB + it * 2 + 3, it)
                step("p6", 1, 0, l * NB + NB)
                step("p7", None, 1, None)
                B.wait_taken(act, ("so", "p7"), l)
                act.activation(hhi[:, 2:6, SEQ:], os_[:, :, :], ACT.Copy).then_inc(cat_hi, 1)

                upto(G0 + 1, l)
                norm(1, l, {1: G0 + 2})

                def gate(tag, it=None):
                    for i in range(4):
                        ft, half = i // 2, i % 2
                        key = ("g", tag, ft, half)
                        B.wait_full(act, key, l, it)
                        for c0, c1, t0 in token_pieces(half):
                            src = bank[B.bank(key)][:, c0:c1]
                            if t0 is None:
                                ins = act.activation(gpad[:, ft, 2 + SEQ:].rearrange("p (b s) -> p b s", b=NB)[:, :, 2:],
                                                     src.rearrange("p (b s) -> p b s", b=NB), ACT.Copy)
                            else:
                                ins = act.activation(gpad[:, ft, 2 + t0:2 + t0 + c1 - c0], src, ACT.Copy)
                        ins.then_inc(B.free[B.bank(key)], 1)

                def silu(done):
                    for ft in range(2):
                        act.wait_ge(gconv, done + ft + 1)
                        act.activation(gact[:, ft, :], gact[:, ft, :], ACT.Silu).then_inc(gsilu, 1)

                gate("pro")
                upto(G0 + 4, l)
                silu(l * (2 * PAIRS))
                upto(G0 + 5, l)
                with act.Fori(0, PAIRS - 1) as it:
                    split_loop(2, l, it)
                    B.wait_room(act, ("d", "loop", 0, 1), l, it)
                    act.activation(guhi[:, :, :], gu[:, :, :], ACT.Copy).then_inc(gu_hi, 1)
                    split_loop(3, l, it)
                    act.wait_ge(glast, l * PAIRS + it + 1)
                    gate("loop", it)
                    split_loop(4, l, it)
                    silu(l * (2 * PAIRS) + it * 2 + 2)
                    for j in (5, 6, 7):
                        split_loop(j, l, it)
                B.wait_room(act, ("d", "end", 0, 1), l)
                act.activation(guhi[:, :, :], gu[:, :, :], ACT.Copy).then_inc(gu_hi, 1)
                for g in range(6):
                    B.wait_full(act, ("last", g), l)
                    act.activation(lrows[:, g * 512:(g + 1) * 512], bank[B.bank(("last", g))][0:NLAST, :],
                                   ACT.Copy).then_inc(B.free[B.bank(("last", g))], 1)
                B.wait_full(act, ("d", "end", 1, 4), l)

        @block.vector
        def _(dve):
            split_to = [0]

            def split(n, l, it=None):
                dve.wait_ge(hi_split, nth(n, l, it))
                s_, w_ = slot(n), width(n)
                dve.tensor_tensor(wlo[:, s_, 0:w_], raw[:, s_, 0:w_], whi[:, s_, 0:w_].bitcast(F32),
                                  ALU.subtract).then_inc(lo_split, 1)

            def upto(n, l):
                while split_to[0] <= n:
                    split(split_to[0], l)
                    split_to[0] += 1

            def lo(out, full_, hi):
                return dve.tensor_tensor(out, full_, hi.bitcast(F32), ALU.subtract)

            def norm(which, l, splits):
                for t in range(TT + 1):
                    if t < TT:
                        if t == 0:
                            dve.wait_ge(gains_in, l * 32 + 16 * (which + 1))
                        dve.wait_ge(rstd, l * (2 * TT) + which * TT + t + 1)
                        dve.scalar_tensor_tensor(out=xn[:, t % 2, :], in0=x[:, t, :], scalar=col(RS + t), in1=gains[:, :],
                                                 op0=ALU.mult, op1=ALU.mult).then_inc(xn_ready, 1)
                    if t > 0:
                        for g in range(2):
                            key = ("hT", which, t - 1, g)
                            dve.wait_ge(h_hi, l * (4 * TT) + which * (2 * TT) + 2 * (t - 1) + g + 1)
                            lo(hlo[:, 4 * g:4 * g + 4, (t - 1) * P:t * P],
                               bank[B.bank(key)][:, :].rearrange("p (k n) -> p k n", k=4),
                               hhi[:, 4 * g:4 * g + 4, (t - 1) * P:t * P]).then_inc(B.free[B.bank(key)], 1)
                    if t in splits:
                        upto(splits[t], l)

            def heads(ap, n=FH):
                return ap.rearrange("p (h d) -> p h d", h=n)

            dve.wait_ge(consts_in, 32)
            dve.wait_ge(pool_const, 1)
            dve.wait_ge(x_in, 16 * TT)
            ident = K("ident")
            dve.tensor_tensor(small[:, 536:544], ident[:, 0:8], ident[:, 32:40], ALU.add)
            dve.drain()
            dve.tensor_copy(sel[:, :, :], small[:, 536:544].unsqueeze(2).to_broadcast([P, FH, P])).then_inc(sel_ready, 1)
            with dve.Fori(0, DEPTH) as l:
                split_to[0] = 0
                norm(0, l, {0: 0, 1: 1, 2: 2})

                z, az, e, u_, lnu, d_, r_, q_, w_, o_ = (n1[:, 40 * i:40 * i + 40] for i in range(10))
                dve.drain()
                B.wait_full(dve, "fl", l)
                dve.wait_ge(foxg_in, l * 64 + 64)
                dve.tensor_tensor(z.rearrange("p (t h) -> p t h", t=TT),
                                  bank[B.bank("fl")][:, 0:40].rearrange("p (t h) -> p t h", t=TT),
                                  fbias[:, :].unsqueeze(1).to_broadcast([P, TT, FH]), ALU.add).then_inc(B.free[B.bank("fl")], 1)
                dve.drain()
                dve.scalar_tensor_tensor(out=az, in0=z, scalar=-1.0, in1=z, op0=ALU.mult, op1=ALU.max).then_inc(fl_z, 1)
                upto(3, l)
                dve.wait_ge(fl_e, l * 2 + 1)
                dve.tensor_scalar(u_, e, 1.0, None, ALU.add).then_inc(fl_z, 1)
                dve.drain()
                dve.tensor_scalar(d_, u_, -1.0, 1e-30, ALU.add, ALU.max)
                dve.tensor_scalar(o_, u_, 1.0, None, ALU.is_equal)
                dve.drain()
                dve.reciprocal(r_, d_)
                dve.drain()
                dve.tensor_tensor(q_, e, r_, ALU.mult)
                dve.tensor_tensor(w_, o_, e, ALU.mult)
                dve.drain()
                dve.wait_ge(fl_e, l * 2 + 2)
                dve.tensor_tensor(q_, lnu, q_, ALU.mult)
                dve.drain()
                dve.tensor_tensor(q_, q_, w_, ALU.add)
                dve.drain()
                dve.scalar_tensor_tensor(out=lf[:, :, :].rearrange("p t h -> p (t h)"), in0=z, scalar=0.0, in1=q_,
                                         op0=ALU.min, op1=ALU.subtract)
                dve.drain()
                dve.tensor_copy(lfx[:, :, 0:8], lf[:, 0:TP, :])
                dve.tensor_copy(lfx[:, :, 32:40], lf[:, 0:TP, :])
                dve.drain().then_inc(lf_ready, 1)

                upto(C0 + 5, l)
                cs = K("cs").rearrange("p (t s d) -> p t s d", t=TT, s=2)
                for t in range(TT):
                    key = ("c", 0, t)
                    dve.drain()
                    B.wait_full(dve, key, l)
                    bk = bank[B.bank(key)]
                    xh = bk[:, :].rearrange("p (h s d) -> p h s d", h=8, s=2)
                    ta = tA[:, 0, :]
                    tb = tA[:, 1, :].rearrange("p (h s d) -> p h s d", h=8, s=2)
                    cos = cs[:, t, 0, :].unsqueeze(1)
                    sin = cs[:, t, 1, :].unsqueeze(1)
                    dve.tensor_tensor(ta.rearrange("p (h d) -> p h d", h=16), bk[:, :].rearrange("p (h d) -> p h d", h=16),
                                      cos.to_broadcast([P, 16, 32]), ALU.mult)
                    dve.tensor_tensor(tb[:, :, 0, :], xh[:, :, 1, :], sin.to_broadcast([P, 8, 32]), ALU.mult)
                    dve.tensor_tensor(tb[:, :, 1, :], xh[:, :, 0, :], sin.to_broadcast([P, 8, 32]),
                                      ALU.mult).then_inc(B.free[B.bank(key)], 1)
                    dve.drain()
                    if t >= 2:
                        dve.wait_ge(kw_ready, l * TT + t - 1)
                        B.wait_full(dve, ("rt", t - 2), l)
                    tav = ta.rearrange("p (h s d) -> p h s d", h=8, s=2)
                    nv = n2[:, t % 2, :].rearrange("p (h s d) -> p h s d", h=8, s=2)
                    dve.tensor_tensor(nv[:, :, 0, :], tav[:, :, 0, :], tb[:, :, 0, :], ALU.subtract)
                    dve.tensor_tensor(nv[:, :, 1, :], tav[:, :, 1, :], tb[:, :, 1, :], ALU.add).then_inc(rot_ready, 1)
                    if t == 1:
                        upto(C0 + 6, l)

                upto(C0 + 10, l)
                dve.wait_ge(dec_in, l * 32 + 32)
                dve.wait_ge(kw_ready, l * TT + TT)
                for n, (h, jb) in enumerate(ret_units()):
                    N = SEQ - P * jb
                    key = ("rs", (h, jb))
                    B.wait_full(dve, key, l)
                    dve.tensor_tensor(ptr[:, n % 3, 0:N], bank[B.bank(key)][:, 0:N], decp[:, h, 0:N],
                                      ALU.mult).then_inc(B.free[B.bank(key)], 1)
                dve.tensor_tensor(qw[:, :, :], rT[:, 0:2, SEQ:], K("qdec").rearrange("p (c n) -> p c n", c=2),
                                  ALU.mult).then_inc(qw_ready, 1)
                for par in range(2):
                    key = f"rss{par}"
                    B.wait_full(dve, key, l)
                    dve.tensor_tensor(ptr[:, 1, :].rearrange("p (c r n) -> p c r n", c=2, r=2)[:, :, par, :],
                                      bank[B.bank(key)][:, 0:2 * P].rearrange("p (c n) -> p c n", c=2),
                                      decs[:, :, :].rearrange("p (c r) n -> p c r n", r=2)[:, :, par, :],
                                      ALU.mult).then_inc(B.free[B.bank(key)], 1)
                for h in range(RH):
                    if h == 2:
                        dve.wait_ge(vm_used, l * 2 + 1)
                    if h == 3:
                        B.wait_full(dve, "rds0", l)
                    dve.tensor_tensor(vm[:, h % 2, :].rearrange("p (b e) -> p b e", b=NB),
                                      rv[:, TS, h * HD:(h + 1) * HD].unsqueeze(1).to_broadcast([P, NB, HD]),
                                      K("bmask")[:, 0:NB].unsqueeze(2).to_broadcast([P, NB, HD]),
                                      ALU.mult).then_inc(vm_ready, 1)
                srcs = ((("ro", 0), 0, 8), (("ro", 1), 8, 8), ("rsoT", 16, 4))

                def group(key, n):
                    return bank[B.bank(key)][:, 0:n * HD].rearrange("p (g d) -> p g d", g=n)

                for key, g0, n in srcs:
                    B.wait_full(dve, key, l)
                    dve.tensor_reduce(col(GS + g0, n), group(key, n), X, ALU.add)
                dve.drain()
                dve.tensor_scalar(col(GM, 20), col(GS, 20), 1.0 / HD, None, ALU.mult)
                dve.drain()
                for key, g0, n in srcs:
                    dve.tensor_tensor(gnd[:, g0:g0 + n, :], group(key, n),
                                      col(GM + g0, n).unsqueeze(2).to_broadcast([P, n, HD]),
                                      ALU.subtract).then_inc(B.free[B.bank(key)], 1)
                dve.drain().then_inc(gn_d, 1)
                dve.wait_ge(s0_in, l * 64 + 64)
                for hp in range(2):
                    key = f"rds{hp}"
                    B.wait_full(dve, key, l)
                    dve.scalar_tensor_tensor(out=s0[:, hp, :], in0=s0[:, hp, :], scalar=K("g16")[:, hp:hp + 1],
                                             in1=bank[B.bank(key)][:, :], op0=ALU.mult,
                                             op1=ALU.add).then_inc(B.free[B.bank(key)], 1)
                dve.drain().then_inc(s_new, 1)
                dve.wait_ge(gn_sq, l + 1)
                dve.tensor_reduce(col(GV, 20), gnsq[:, :, :], X, ALU.add).then_inc(gn_v, 1)
                dve.wait_ge(gn_r, l + 1)
                dve.tensor_tensor(gnsq[:, :, :], gnd[:, :, :], col(GR, 20).unsqueeze(2).to_broadcast([P, 20, HD]), ALU.mult)
                dve.drain()
                dve.wait_ge(gs_ready, l + 1)
                dve.tensor_tensor(gs[:, :, :].rearrange("p t c -> p (t c)"), gnsq[:, :, :].rearrange("p g d -> p (g d)"),
                                  gs[:, :, :].rearrange("p t c -> p (t c)"), ALU.mult).then_inc(oret, 1)

                for c in (2, 3):
                    i = c - 2
                    k_ = C0 + 4 * c + 3
                    upto(k_ + 2, l)
                    gain = fqg if c == 2 else fkg
                    for t in range(TT + 1):
                        if t < TT:
                            dve.wait_ge(fsq, l * (2 * TT) + i * TT + t + 1)
                            dve.tensor_reduce(col(FSS[i] + 8 * t, 8), heads(tA[:, t % 2, :]), X, ALU.add).then_inc(fss, 1)
                        if t > 0:
                            s_ = t - 1
                            key = ("c", c, s_)
                            dve.drain()
                            dve.wait_ge(frs, l * (2 * TT) + i * TT + s_ + 1)
                            dve.tensor_tensor(heads(n1[:, :]), heads(bank[B.bank(key)][:, :]),
                                              col(FRS[i] + 8 * s_, 8).unsqueeze(2).to_broadcast([P, FH, HD]),
                                              ALU.mult).then_inc(B.free[B.bank(key)], 1)
                            dve.drain()
                            if s_ >= 2:
                                B.wait_full(dve, ("qT" if c == 2 else "kT", s_ - 2), l)
                                if c == 3:
                                    wait_k_stored(dve, s_ - 2, l)
                            elif s_ == 0:
                                if c == 2:
                                    dve.wait_ge(kw_ready, l * TT + TT)
                                else:
                                    B.wait_full(dve, ("qT", TT - 1), l)
                            dve.tensor_tensor(n2[:, s_ % 2, :], n1[:, :], gain[:, :], ALU.mult).then_inc(fn_ready, 1)
                        if t == 2:
                            upto(k_ + 3, l)
                    if c == 2:
                        dve.tensor_tensor(lexp[:, :].rearrange("p (b h) -> p b h", h=FH),
                                          lf[:, TS, :].unsqueeze(1).to_broadcast([P, 16, FH]),
                                          K("bmask").unsqueeze(2).to_broadcast([P, 16, FH]), ALU.mult).then_inc(lexp_ready, 1)
                        dve.wait_ge(nct_ready, l * 3 + 1)
                        dve.scalar_tensor_tensor(out=ncp[32:40, :], in0=bank[B.bank("cs")][32:40, :], scalar=-1.0,
                                                 in1=nct[32:40, :].bitcast(F32), op0=ALU.mult,
                                                 op1=ALU.subtract).then_inc(B.free[B.bank("cs")], 1)
                        dve.wait_ge(nct_ready, l * 3 + 2)
                        dve.tensor_copy(ctot[:, :], bank[B.bank("cc")][:, PAST - 1:PAST])
                        dve.scalar_tensor_tensor(out=ncc[64:128, :], in0=bank[B.bank("cc")][64:128, :], scalar=-1.0,
                                                 in1=nct[64:128, :].bitcast(F32), op0=ALU.mult,
                                                 op1=ALU.subtract).then_inc(B.free[B.bank("cc")], 1)
                        dve.drain()
                        B.wait_full(dve, "cn", l)
                        dve.tensor_scalar(wcn[:, :], bank[B.bank("cn")][:, 0:P], ctot[:, 0:1], -1.0, ALU.add,
                                          ALU.mult).then_inc(B.free[B.bank("cn")], 1)
                        dve.drain().then_inc(wcn_ready, 1)
                        dve.wait_ge(nct_ready, l * 3 + 3)
                        lo(ncn[64:128, :], wcn[64:128, :], wcnh[64:128, :]).then_inc(nc_ready, 1)
                    upto(k_ + 4, l)
                upto(C0 + 19 + 4, l)

                def by_batch(ap):
                    return ap.rearrange("p (b s) -> p b s", b=NB)

                def mul_bank(out_of, key, other):
                    ft, half = key[-2:]
                    for c0, c1, t0 in token_pieces(half):
                        src = bank[B.bank(key)][:, c0:c1]
                        t1 = None if t0 is None else t0 + c1 - c0
                        ins = dve.tensor_tensor(out_of(ft, t0, t1), by_batch(src) if t0 is None else src, other(ft, t0, t1),
                                                ALU.mult)
                    return ins

                def plain(buf):
                    return lambda ft, t0, t1: by_batch(buf[:, ft, SEQ:]) if t0 is None else buf[:, ft, t0:t1]

                def in_padded(buf):
                    return lambda ft, t0, t1: (by_batch(buf[:, ft, 2 + SEQ:])[:, :, 2:] if t0 is None
                                               else buf[:, ft, 2 + t0:2 + t1])

                def conv_out(buf):
                    return lambda ft, t0, t1: (by_batch(buf[:, ft, NY - NB * (NS + 2):NY])[:, :, 2:] if t0 is None
                                               else buf[:, ft, t0:t1])

                def conv(out, u, ft, tap):
                    ins = dve.tensor_scalar(out[:, ft, 0:NY], u[:, ft, 0:NY], tap(0), None, ALU.mult)
                    for j in (1, 2):
                        dve.drain()
                        ins = dve.scalar_tensor_tensor(out=out[:, ft, :], in0=u[:, ft, j:j + NY], scalar=tap(j),
                                                       in1=out[:, ft, :], op0=ALU.mult, op1=ALU.add)
                    return ins

                dve.wait_ge(hist_u, l + 1)
                wait_k_stored(dve, TT - 2, l)
                wait_k_stored(dve, TT - 1, l)
                for i in range(4):
                    key = ("ch_", i // 2, i % 2)
                    B.wait_full(dve, key, l)
                    B.wait_taken(dve, ("cc_", i // 2, i % 2), l)
                    mul_bank(in_padded(upad), key, plain(ccs)).then_inc(B.free[B.bank(key)], 1)
                dve.drain().then_inc(u_ready, 1)
                upto(CH + 3, l)
                B.wait_taken(dve, "taps", l)
                for ft in range(2):
                    conv(ycv, upad, ft, lambda j: taps[:, ft, 16 + j:17 + j])
                dve.drain()
                for i in range(4):
                    key = ("cb_", i // 2, i % 2)
                    B.wait_full(dve, key, l)
                    mul_bank(plain(oc), key, conv_out(ycv)).then_inc(B.free[B.bank(key)], 1)
                upto(WO + 2, l)
                dve.wait_ge(cat_hi, l * HIS + 1)
                lo(hlo[:, 6:8, :], oc[:, :, :], hhi[:, 6:8, :]).then_inc(cat_lo, 1)

                units = fox_units()
                NU = len(units)
                for n in range(NU + 4):
                    if n < NU:
                        h, qb = units[n]
                        B.wait_full(dve, ("fs", h, qb), l)
                        dve.tensor_reduce(col(NM + n), bank[B.bank(("fs", h, qb))][:, 0:P * (qb + 1)], X, ALU.max,
                                          negate=True).then_inc(nmax, 1)
                    if 1 <= n < NU + 1:
                        m = n - 1
                        h, qb = units[m]
                        N = P * (qb + 1)
                        B.wait_taken(dve, ("fs", h, qb), l)
                        dve.reciprocal(col(REC + m), col(RSUM + m))
                        dve.drain()
                        dve.tensor_scalar(pf[:, m % 3, 0:N], pf[:, m % 3, 0:N], col(REC + m), None, ALU.mult).then_inc(pnorm, 1)
                    if n >= 4:
                        h, qb = units[n - 4]
                        if h % 2 and qb == TP - 1:
                            key = ("fo", h // 2)
                            dve.wait_ge(cat_hi, l * HIS + 2 + h // 2)
                            lo(hlo[:, 2 + h // 2, 0:SEQ], bank[B.bank(key)][:, :],
                               hhi[:, 2 + h // 2, 0:SEQ]).then_inc(B.free[B.bank(key)], 1)
                for g in range(3):
                    w_ = 256 if g < 2 else P
                    key = ("orT", g)
                    dve.wait_ge(cat_hi, l * HIS + 6 + g)
                    lo(hlo[:, 0:2, 256 * g:256 * g + w_], bank[B.bank(key)][:, :].rearrange("p (r c) -> p r c", r=2)[:, :, 0:w_],
                       hhi[:, 0:2, 256 * g:256 * g + w_]).then_inc(B.free[B.bank(key)], 1)

                def step(tag, ahead, now, b, it=None):
                    if ahead is not None:
                        for p_ in (1, 3):
                            key = ("kt", tag, p_)
                            B.wait_full(dve, key, l, it)
                            dve.tensor_copy(kT[:, p_, :], bank[B.bank(key)][:, :]).then_inc(B.free[B.bank(key)], 1)
                        o = SB + 8 * ahead
                        for key, n_, c_ in ((("ss", tag), 512, 0), (("sn", tag), P, 1)):
                            B.wait_full(dve, key, l, it)
                            dve.tensor_reduce(col(o + c_), bank[B.bank(key)][:, 0:n_], X, ALU.max, negate=True)
                        dve.drain()
                        dve.tensor_tensor(col(o + 2), col(o), col(o + 1), ALU.min).then_inc(smax, 1)
                        B.wait_taken(dve, ("ss", tag), l, it)
                        B.wait_taken(dve, ("sn", tag), l, it)
                        dve.tensor_tensor(col(o + 5), col(o + 3), col(o + 4), ALU.add)
                        dve.drain()
                        dve.reciprocal(col(o + 6), col(o + 5))
                        dve.drain()
                        dve.tensor_scalar(ps[:, ahead, :], ps[:, ahead, :], col(o + 6), None, ALU.mult).then_inc(snorm, 1)
                    if now is not None:
                        key = ("pt", tag, 1)
                        B.wait_full(dve, key, l, it)
                        dve.tensor_copy(pTs[:, now, 512:640], bank[B.bank(key)][:, 0:P]).then_inc(B.free[B.bank(key)], 1)
                        key = ("so", tag)
                        B.wait_full(dve, key, l, it)
                        for par in range(2):
                            src = bank[B.bank(key)][64 * par:64 * par + 64, 0:P].rearrange("p (c s) -> p c s", c=4)
                            ins = dve.tensor_copy(os_[64 * par:64 * par + 64, :, bass.ds(b * 16, 16)],
                                                  src[:, :, 16 * par:16 * par + 16])
                        ins.then_inc(B.free[B.bank(key)], 1)

                step("pro", 0, None, 0)
                with dve.Fori(0, STEPS) as it:
                    step("b0", 1, 0, it * 2, it)
                    step("b1", 0, 1, it * 2 + 1, it)
                step("p6", 1, 0, 6)
                step("p7", None, 1, 7)
                dve.drain()
                dve.wait_ge(cat_hi, l * HIS + HIS)
                lo(hlo[:, 2:6, SEQ:], os_[:, :, :], hhi[:, 2:6, SEQ:]).then_inc(cat_lo, 1)

                def add(key, c, t, it=None):
                    B.wait_full(dve, key, l, it)
                    dve.tensor_tensor(x[:, t, 512 * c:512 * c + 512], x[:, t, 512 * c:512 * c + 512],
                                      bank[B.bank(key)][:, :], ALU.add).then_inc(B.free[B.bank(key)], 1)

                for c in range(2):
                    upto(WO + 4 * c + 5, l)
                    for t in range(TT):
                        add(("wo", c, t), c, t)
                        if c == 1:
                            dve.drain().then_inc(x_done, 1)
                        elif t == 1:
                            upto(WO + 6, l)

                norm(1, l, {1: G0 + 2})
                upto(G0 + 3, l)

                def gate_conv(tag, ft, it=None):
                    if ft == 0:
                        dve.drain()
                        for i in range(4):
                            B.wait_taken(dve, ("g", tag, i // 2, i % 2), l, it)
                        dve.wait_ge(gpad_hist, l * PAIRS + 1 if it is None else l * PAIRS + it + 2)
                    conv(gact, gpad, ft, lambda j: ftap[:, ft, j:j + 1]).then_inc(gconv, 1)

                def product(wait, done):
                    dve.drain()
                    dve.wait_ge(gsilu, done)
                    for i in range(4):
                        wait(i)
                        mul_bank(plain(gu), ("u", "pro", i // 2, i % 2), conv_out(gact)).then_inc(B.free[U_BANKS[i]], 1)

                gate_conv("pro", 0)
                upto(G0 + 4, l)
                gate_conv("pro", 1)
                upto(G0 + 5, l)
                with dve.Fori(0, PAIRS - 1) as it:
                    product(lambda i: B.wait_full_before(dve, ("d", "loop", 0, U_BANKS[i] - 4), l, it),
                            l * (2 * PAIRS) + it * 2 + 2)
                    split(LOOP0 + 2, l, it)
                    dve.wait_ge(gu_hi, l * PAIRS + it + 1)
                    lo(gulo[:, :, :], gu[:, :, :], guhi[:, :, :]).then_inc(gu_ready, 1)
                    split(LOOP0 + 3, l, it)
                    gate_conv("loop", 0, it)
                    split(LOOP0 + 4, l, it)
                    for n in range(2 * TT):
                        add(("d", "loop", n // TT, n % TT), n // TT, n % TT, it)
                        if n == 2:
                            gate_conv("loop", 1, it)
                        if n == 4:
                            split(LOOP0 + 5, l, it)
                    dve.drain()
                    split(LOOP0 + 6, l, it)
                    split(LOOP0 + 7, l, it)
                product(lambda i: B.wait_full_before(dve, ("d", "end", 0, U_BANKS[i] - 4), l),
                        l * (2 * PAIRS) + 2 * PAIRS)
                dve.wait_ge(gu_hi, l * PAIRS + PAIRS)
                lo(gulo[:, :, :], gu[:, :, :], guhi[:, :, :]).then_inc(gu_ready, 1)
                for n in range(2 * TT):
                    add(("d", "end", n // TT, n % TT), n // TT, n % TT)
                    if n >= TT:
                        dve.drain().then_inc(x_done, 1)

        @block.tensor
        def _(pe):
            ident = K("ident")
            identb = maskb[:, 0:P]

            def mm(out, lhsT, rhs, start, stop):
                return pe.matmul(out, lhsT=lhsT, rhs=rhs, start=start, stop=stop, skip_group_check=True)

            def mm3(out, lh, ll, rh, rl, start, stop):
                mm(out, lh, rh, start, False)
                mm(out, lh, rl, False, False)
                return mm(out, ll, rh, False, stop)

            def fill(ins, key):
                ins.then_inc(B.full[B.bank(key)], 1)

            def ready(n, l, it=None):
                pe.wait_ge(lo_split, nth(n, l, it, SLOTS + 1))

            def wait_h(which, l, t):
                for g in range(2):
                    B.wait_taken(pe, ("hT", which, t, g), l)

            def tm_slab(n, i, last_, acts, nk, kbase, keys, l, it=None):
                ready(n, l, it)
                s_ = slot(n)
                hi, lo_ = acts
                for t in range(TT):
                    out = bank[B.bank(keys[t])][:, :]
                    if i == 0:
                        B.wait_room(pe, keys[t], l, it)
                    for k in range(nk):
                        ts = slice(t * P, t * P + P)
                        ins = mm3(out, hi[:, kbase + k, ts], lo_[:, kbase + k, ts], whi[:, s_, 512 * k:512 * k + 512],
                                  wlo[:, s_, 512 * k:512 * k + 512], i == 0 and k == 0, last_ and k == nk - 1)
                    if last_:
                        fill(ins, keys[t])
                if not last_:
                    ins.then_inc(slab_used, 1)

            def fm_job(n0, keys, l, it=None):
                for i in range(2):
                    ready(n0 + i, l, it)
                    s_ = slot(n0 + i)
                    for key in keys:
                        ft, half = key[-2:]
                        out = bank[B.bank(key)][:, 0:HALF]
                        if i == 0:
                            B.wait_room(pe, key, l, it)
                        for k in range(4):
                            ws = slice(256 * k + P * ft, 256 * k + P * ft + P)
                            ts = slice(half * HALF, half * HALF + HALF)
                            ins = mm3(out, whi[:, s_, ws], wlo[:, s_, ws], hhi[:, 4 * i + k, ts], hlo[:, 4 * i + k, ts],
                                      i == 0 and k == 0, i == 1 and k == 3)
                        if i == 1:
                            fill(ins, key)
                    if i == 0:
                        ins.then_inc(slab_used, 1)

            def transposes(key, parts, l, it=None):
                B.wait_room(pe, key, l, it)
                if parts[0][1].shape[0] < P:
                    apart(pe)
                for dst, src in parts:
                    ins = pe.transpose(dst, src, ident[0:src.shape[0], 0:src.shape[0]])
                fill(ins, key)

            def norm(which, l):
                for t in range(TT):
                    pe.wait_ge(xn_ready, l * (2 * TT) + which * TT + t + 1)
                    for g in range(2):
                        key = ("hT", which, t, g)
                        bk = bank[B.bank(key)]
                        transposes(key, [(bk[:, k * P:k * P + P], xn[:, t % 2, (4 * g + k) * P:(4 * g + k + 1) * P])
                                         for k in range(4)], l)

            def turn(name, src, t, l):
                key = (name, t)
                bk = bank[B.bank(key)]
                transposes(key, [(bk[:, k * P:k * P + P], src[:, k * P:k * P + P]) for k in range(4)], l)

            def chunk(c, l):
                for i in range(4):
                    tm_slab(C0 + 4 * c + i, i, i == 3, (hhi, hlo), 2, 2 * i, [("c", c, t) for t in range(TT)], l)

            pe.wait_ge(consts_in, 32)
            pe.wait_ge(pool_const, 1)
            pe.wait_ge(sel_ready, 1)
            with pe.Fori(0, DEPTH) as l:
                norm(0, l)
                B.wait_room(pe, "fl", l)
                for i in range(2):
                    ready(FL + i, l)
                    for t in range(TT):
                        if i == 0:
                            wait_h(0, l, t)
                        for k in range(4):
                            ws = slice(k * FH, k * FH + FH)
                            ts = slice(t * P, t * P + P)
                            s_ = slot(FL + i)
                            ins = mm3(bank[B.bank("fl")][:, t * FH:t * FH + FH], hhi[:, 4 * i + k, ts], hlo[:, 4 * i + k, ts],
                                      whi[:, s_, ws], wlo[:, s_, ws], i == 0 and t == 0 and k == 0, i == 1 and t == TT - 1 and k == 3)
                    if i == 0:
                        ins.then_inc(slab_used, 1)
                fill(ins, "fl")
                chunk(0, l)
                pe.wait_ge(rows_in, l * 64 + 64)
                transposes("taps", [(bank[B.bank("taps")][:, c * NTAP:(c + 1) * NTAP], rows[:, c * P:(c + 1) * P])
                                    for c in range(NCT)], l)
                for t in range(TT):
                    pe.wait_ge(rot_ready, l * TT + t + 1)
                    turn("rt", n2[:, t % 2, :], t, l)
                chunk(1, l)

                B.wait_all_taken(pe, [("rt", t) for t in range(TT)] + [("c", 1, t) for t in range(TT)], l)
                units = ret_units()
                for n in range(len(units) + 1):
                    if n < len(units):
                        h, jb = units[n]
                        r0 = 64 * (h % 2)
                        key = ("rs", (h, jb))
                        B.wait_room(pe, key, l)
                        fill(mm(bank[B.bank(key)][:, 0:SEQ - P * jb], rT[r0:r0 + 64, 2 + h // 2, jb * P:jb * P + P],
                                rT[r0:r0 + 64, h // 2, jb * P:SEQ], True, True), key)
                    if n > 0:
                        m = n - 1
                        h, jb = units[m]
                        B.wait_taken(pe, ("rs", (h, jb)), l)
                        if m == 0:
                            B.wait_room(pe, ("ro", 0), l)
                            B.wait_room(pe, ("ro", 1), l)
                        for ib in range(jb, TP):
                            c0 = (ib % 2) * 256 + h * HD
                            key = ("ro", ib // 2)
                            ins = mm(bank[B.bank(key)][:, c0:c0 + HD], ptr[:, m % 3, (ib - jb) * P:(ib - jb + 1) * P],
                                     rv[:, jb, h * HD:(h + 1) * HD], m == 0 and ib % 2 == 0, h == RH - 1 and ib == jb)
                            if h == RH - 1 and ib == jb and ib % 2:
                                fill(ins, key)
                pe.wait_ge(kw_ready, l * TT + TT)
                B.wait_room(pe, "rst", l)
                for h in range(RH):
                    r0 = 64 * (h % 2)
                    for t in range(TP):
                        ins = mm(bank[B.bank("rst")][r0:r0 + 64, (h // 2) * HD:(h // 2 + 1) * HD], kw[:, t, h * HD:(h + 1) * HD],
                                 rv[:, t, h * HD:(h + 1) * HD], t == 0, t == TP - 1)
                fill(ins, "rst")
                for par in range(2):
                    r0 = 64 * par
                    key = f"rss{par}"
                    B.wait_room(pe, key, l)
                    for hp in range(2):
                        ins = mm(bank[B.bank(key)][:, hp * P:(hp + 1) * P], rT[r0:r0 + 64, 2 + hp, SEQ:],
                                 rT[r0:r0 + 64, hp, SEQ:], True, True)
                    fill(ins, key)
                for h in range(RH):
                    r0 = 64 * (h % 2)
                    key = f"rds{h // 2}"
                    pe.wait_ge(vm_ready, l * RH + h + 1)
                    if h % 2 == 0:
                        B.wait_room(pe, key, l)
                    ins = mm(bank[B.bank(key)][r0:r0 + 64, :], kw[:, TS, h * HD:(h + 1) * HD], vm[:, h % 2, :], True, True)
                    if h % 2 == 0:
                        ins.then_inc(vm_used, 1)
                    else:
                        fill(ins, key)
                pe.wait_ge(qw_ready, l + 1)
                pe.wait_ge(s0_in, l * 64 + 64)
                for par in range(2):
                    B.wait_taken(pe, f"rss{par}", l)
                B.wait_room(pe, "rso", l)
                for h in range(RH):
                    r0 = 64 * (h % 2)
                    out = bank[B.bank("rso")]
                    c0 = (h // 2) * P
                    mm(out[r0:r0 + 64, c0:c0 + P], rv[:, TS, h * HD:(h + 1) * HD], ptr[:, 1, h * P:(h + 1) * P], h < 2, False)
                    for b in range(NB):
                        ins = mm(out[r0:r0 + 64, c0 + b * NS:c0 + (b + 1) * NS], s0[r0:r0 + 64, h // 2, b * HD:(b + 1) * HD],
                                 qw[r0:r0 + 64, h // 2, b * NS:(b + 1) * NS], False, b == NB - 1)
                fill(ins, "rso")
                B.wait_taken(pe, "rso", l)
                transposes("rsoT", [(bank[B.bank("rsoT")][:, hp * P:(hp + 1) * P], rso[:, hp * P:(hp + 1) * P])
                                    for hp in range(2)], l)

                chunk(2, l)
                for t in range(TT):
                    pe.wait_ge(fn_ready, l * (2 * TT) + t + 1)
                    turn("qT", n2[:, t % 2, :], t, l)
                pe.wait_ge(lf_ready, l + 1)
                B.wait_room(pe, "cs", l)
                for i in range(TP):
                    ins = mm(bank[B.bank("cs")][0:40, :], lfx[:, i, :], K("tri")[:, 384 - P * i:896 - P * i], i == 0, i == TP - 1)
                fill(ins, "cs")
                pe.wait_ge(lcd_ready, l + 1)
                B.wait_room(pe, "cc", l)
                for i in range(TP):
                    ins = mm(bank[B.bank("cc")][:, :], lcd[:, i, :, :].rearrange("p a b -> p (a b)"),
                             K("tri")[:, 384 - P * i:896 - P * i], i == 0, i == TP - 1)
                fill(ins, "cc")
                pe.wait_ge(lexp_ready, l + 1)
                B.wait_room(pe, "cn", l)
                fill(mm(bank[B.bank("cn")][:, 0:P], lexp[:, :], K("tris"), True, True), "cn")
                chunk(3, l)
                for t in range(TT):
                    pe.wait_ge(fn_ready, l * (2 * TT) + TT + t + 1)
                    turn("kT", n2[:, t % 2, :], t, l)
                chunk(4, l)
                for first, name in ((CC, "cc_"), (CH, "ch_"), (CB, "cb_")):
                    fm_job(first, [(name, i // 2, i % 2) for i in range(4)], l)

                pe.wait_ge(nc_ready, l + 1)
                B.wait_all_taken(pe, [(name, t) for name in ("qT", "kT") for t in range(TT)]
                                 + [("c", 4, t) for t in range(TT)], l)
                units = fox_units()
                NU = len(units)
                for n in range(NU + 3):
                    if n < NU:
                        h, qb = units[n]
                        r0, N = 64 * (h % 2), P * (qb + 1)
                        key = ("fs", h, qb)
                        out = bank[B.bank(key)]
                        B.wait_room(pe, key, l)
                        mm(out[:, 0:N], fqT[r0:r0 + 64, h // 2, qb * P:(qb + 1) * P], fkT[r0:r0 + 64, h // 2, 0:N], True, False)
                        mm(out[:, 0:N], sel[:, h, :], ncp[:, 0:N], False, False)
                        fill(mm(out[:, N - P:N], identb, maskb[:, P:2 * P], False, True), key)
                    if 2 <= n < NU + 2:
                        m = n - 2
                        h, qb = units[m]
                        key = ("ft", h, qb)
                        pe.wait_ge(pnorm, l * NU + m + 1)
                        bk = bank[B.bank(key)]
                        transposes(key, [(bk[:, k * P:(k + 1) * P], pf[:, m % 3, k * P:(k + 1) * P]) for k in range(qb + 1)], l)
                    if n >= 3:
                        m = n - 3
                        h, qb = units[m]
                        r0 = 64 * (h % 2)
                        key = ("fo", h // 2)
                        B.wait_taken(pe, ("ft", h, qb), l)
                        if h % 2 == 0 and qb == 0:
                            B.wait_room(pe, key, l)
                        for k in range(qb + 1):
                            ins = mm(bank[B.bank(key)][r0:r0 + 64, qb * P:(qb + 1) * P], fv[:, k, h * HD:(h + 1) * HD],
                                     pTf[:, m % 2, k * P:(k + 1) * P], k == 0, k == qb)
                        if h % 2 and qb == TP - 1:
                            fill(ins, key)
                pe.wait_ge(oret, l + 1)
                for g in range(3):
                    bk = bank[B.bank(("orT", g))]
                    transposes(("orT", g), [(bk[:, r * 256 + (t % 2) * P:r * 256 + (t % 2) * P + P], gs[:, t, r * P:(r + 1) * P])
                                            for t in range(2 * g, min(2 * g + 2, TT)) for r in range(2)], l)

                def step(tag, ahead, now, b, it=None):
                    if ahead is not None:
                        pe.wait_ge(k_in, (l * NB + b + 1) * 16)
                        for p_ in range(4):
                            key = ("kt", tag, p_)
                            bk = bank[B.bank(key)]
                            transposes(key, [(bk[:, k * P:(k + 1) * P], kb[:, k, p_ * P:(p_ + 1) * P]) for k in range(4)], l, it)
                        pe.wait_ge(q_ready, l * NB + b + 1)
                        for p_ in (2, 3):
                            B.wait_taken(pe, ("kt", tag, p_), l, it)
                        for name, keys_, sums, n_ in (("ss", lambda p_: kT[:, p_, :], ncc[:, :], PAST),
                                                      ("sn", lambda p_: fkT[:, p_, SEQ:], ncn[:, :], P)):
                            key = (name, tag)
                            out = bank[B.bank(key)][:, 0:n_]
                            B.wait_room(pe, key, l, it)
                            for p_ in range(4):
                                mm(out, qbd[:, ahead, p_ * P:(p_ + 1) * P], keys_(p_), p_ == 0, False)
                            ins = mm(out, eb[:, ahead, :], sums, False, name == "ss")
                            if name == "sn":
                                ins = mm(out, identb, maskb[:, bass.ds(b * P + 2 * P, P)], False, True)
                            fill(ins, key)
                    if now is not None:
                        nb = b if ahead is None else b - 1
                        pe.wait_ge(snorm, l * NB + nb + 1)
                        for g, ks in enumerate((range(4), range(4, 5))):
                            key = ("pt", tag, g)
                            bk = bank[B.bank(key)]
                            transposes(key, [(bk[:, (k % 4) * P:(k % 4 + 1) * P], ps[:, now, k * P:(k + 1) * P]) for k in ks], l, it)
                        pe.wait_ge(v_in[now], l * 64 + ((nb // 2 + 1) * 16 if it is None else it * 16 + 16))
                        B.wait_taken(pe, ("pt", tag, 0), l, it)
                        B.wait_taken(pe, ("pt", tag, 1), l, it)
                        key = ("so", tag)
                        B.wait_room(pe, key, l, it)
                        for p_ in range(4):
                            for k in range(5):
                                v = vb[:, now, k, p_ * P:(p_ + 1) * P] if k < 4 else fv[:, TS, p_ * P:(p_ + 1) * P]
                                ins = mm(bank[B.bank(key)][:, p_ * 32:(p_ + 1) * 32], v,
                                         pTs[:, now, k * P + 32 * p_:k * P + 32 * p_ + 32], k == 0, k == 4)
                        fill(ins, key)

                step("pro", 0, None, 0)
                with pe.Fori(0, STEPS) as it:
                    step("b0", 1, 0, it * 2 + 1, it)
                    step("b1", 0, 1, it * 2 + 2, it)
                step("p6", 1, 0, NB - 1)
                step("p7", None, 1, NB - 1)

                pe.wait_ge(cat_lo, l * CATS + CATS)
                B.wait_all_taken(pe, [("fo", p_) for p_ in range(4)] + [("orT", g) for g in range(3)], l)
                for c in range(2):
                    for i in range(4):
                        tm_slab(WO + 4 * c + i, i, i == 3, (hhi, hlo), 2, 2 * i, [("wo", c, t) for t in range(TT)], l)

                norm(1, l)
                for t in range(TT):
                    wait_h(1, l, t)
                fm_job(G0, [("g", "pro", i // 2, i % 2) for i in range(4)], l)
                fm_job(G0 + 2, [("u", "pro", i // 2, i % 2) for i in range(4)], l)

                def down(first, tag, it=None):
                    for c in range(2):
                        tm_slab(first + c, 0, True, (guhi, gulo), 2, 0, [("d", tag, c, t) for t in range(TT)], l, it)

                with pe.Fori(0, PAIRS - 1) as it:
                    fm_job(LOOP0, [("g", "loop", i // 2, i % 2) for i in range(4)], l, it)
                    pe.wait_ge(gu_ready, l * PAIRS + it + 1)
                    down(LOOP0 + 2, "loop", it)
                    fm_job(LOOP0 + 4, [("u", "loop", i // 2, i % 2) for i in range(4)], l, it)
                pe.wait_ge(gu_ready, l * PAIRS + PAIRS)
                down(DLAST, "end")
                pe.wait_ge(glast, l * PAIRS + PAIRS)
                for g in range(6):
                    bk = bank[B.bank(("last", g))]
                    transposes(("last", g), [(bk[0:NLAST, k * P:(k + 1) * P], last[:, 4 * g + k, :]) for k in range(4)], l)


INS = ("x_prompt", "x_sample", "cache_fox_k", "cache_fox_v", "cache_fox_logf", "state_ret", "state_conv",
       "state_ffn_conv", "norm_mix", "w_in", "ret_gn_gain", "fox_q_gain", "fox_k_gain", "fox_f_bias", "conv_w",
       "w_out", "norm_ffn", "w_gate", "w_up", "ffn_conv_w", "w_down")
OUTS = (("y_prompt", (1, SEQ, D)), ("y_sample", (NB, NS, D)),
        ("p_fox_k", (DEPTH, 1, SEQ, FH, HD)), ("p_fox_v", (DEPTH, 1, SEQ, FH, HD)), ("p_fox_logf", (DEPTH, 1, SEQ, FH)),
        ("p_ret", (DEPTH, 1, RH, HD, HD)), ("p_conv", (DEPTH, 1, 2, CW)), ("p_ffn", (DEPTH, 1, 2, DFF)),
        ("s_fox_k", (DEPTH, NB, NS, FH, HD)), ("s_fox_v", (DEPTH, NB, NS, FH, HD)), ("s_fox_logf", (DEPTH, NB, NS, FH)),
        ("s_ret", (DEPTH, NB, RH, HD, HD)), ("s_conv", (DEPTH, NB, 2, CW)), ("s_ffn", (DEPTH, NB, 2, DFF)))


def kernel(**inputs):
    import ml_dtypes
    from concourse import bacc
    from concourse.bass_utils import run_bass_kernel_spmd

    nc = bacc.Bacc("TRN2", target_bir_lowering=False, num_devices=1, dynamic_dma_scratch_size=1024)
    c_tables, c_decay, c_masks = tables()
    arrays = {name: np.ascontiguousarray(inputs[name]) for name in INS}
    arrays.update(c_tables=c_tables, c_decay=c_decay, c_masks=c_masks.astype(ml_dtypes.bfloat16))
    types = {"c_masks": BF16}
    a = {name: nc.dram_tensor("in_" + name, list(v.shape), types.get(name, F32), kind="ExternalInput").ap()
         for name, v in arrays.items()}
    for name, shape in OUTS:
        a[name] = nc.dram_tensor("out_" + name, list(shape), F32, kind="ExternalOutput").ap()
    build(nc, a)
    res = run_bass_kernel_spmd(nc, [{"in_" + name: v for name, v in arrays.items()}], core_ids=[0])
    return tuple(res.results[0]["out_" + name] for name, _ in OUTS)
```

```python
from contextlib import ExitStack

import numpy as np

import concourse.bass as bass
from concourse import mybir

F32 = mybir.dt.float32
F32R = mybir.dt.float32r
BF16 = mybir.dt.bfloat16
ACT = mybir.ActivationFunctionType
ALU = mybir.AluOpType
X = mybir.AxisListType.X

P = 128
D = 1024
KT = D // P
SEQ, NB, NS, PAST = 512, 8, 16, 512
NTOK = SEQ + NB * NS
TT = NTOK // P
TP = SEQ // P
TS = TP
DEPTH = 2
RH, HD, FH = 4, 64, 8
RW, FW, CW = RH * HD, FH * HD, 256
DFF = 2816
PAIRS = DFF // 256
COL_FL = 4 * RW + 3 * FW
COL_CONV = COL_FL + FH
PROJ = COL_CONV + 3 * CW
EPS = 1e-6
HALF = NTOK // 2
PADDED = 2 + SEQ + NB * (NS + 2)
NY = PADDED - 2
NTAP = NB * 2 + 3
NLAST = 2 + NB * 2
NCT = 2 + DFF // P
NEG = -1e30
SLOTS = 3

FL, CC, CH, CB, WO, G0 = 4, 22, 24, 26, 28, 36
C0 = 2
SLABS = G0 + 4 + 6 * (PAIRS - 1) + 2
LOOP0 = G0 + 4
DLAST = SLABS - 2
assert SLABS % SLOTS == 0 and 6 % SLOTS == 0

CONST = {}
_at = 0
for _name, _n in (("ident", P), ("cs", TT * 64), ("kdec", TT * RH), ("qdec", 2 * P), ("g16", 2), ("tri", 896),
                  ("tris", P), ("bmask", 16), ("e0", P), ("bsel", NB)):
    CONST[_name] = (_at, _n)
    _at += _n
NCONST = _at


def tables():
    p = np.arange(P)
    gamma = 1.0 - 2.0 ** (-5.0 - np.arange(RH))
    c = np.zeros((P, NCONST), np.float32)

    def put(name, a):
        o, n = CONST[name]
        c[:, o:o + n] = np.asarray(a).reshape(P, n)

    put("ident", np.eye(P))
    pos = np.stack([t * P + p for t in range(TP)] + [PAST + p % NS], 1)
    inv = np.float32(10000.0) ** (-np.arange(HD // 2, dtype=np.float32) / (HD // 2))
    ang = (pos.astype(np.float32)[:, :, None] * inv[None, None, :].astype(np.float32)).astype(np.float64)
    put("cs", np.stack([np.cos(ang), np.sin(ang)], 2))
    left = np.stack([SEQ - 1 - (t * P + p) for t in range(TP)] + [NS - 1 - p % NS], 1)
    put("kdec", gamma[None, None, :] ** left[:, :, None] * HD ** -0.5)
    par = p // HD
    put("qdec", np.stack([gamma[2 * hp + par][:, None] ** (p[None, :] % NS + 1) for hp in range(2)], 1))
    put("g16", np.stack([gamma[2 * hp + par] ** NS for hp in range(2)], 1))
    put("tri", (np.arange(896)[None, :] - 384) >= p[:, None])
    same = (p[:, None] // NS) == (p[None, :] // NS)
    put("tris", same & (p[:, None] <= p[None, :]))
    b8 = np.arange(NB)
    put("bmask", np.tile((p // NS)[:, None] == b8[None, :], (1, 2)))
    put("e0", (p[:, None] % FH) == (p[None, :] // NS))
    put("bsel", ((p % HD) // FH)[:, None] == b8[None, :])
    i = np.arange(SEQ)
    dp = np.where(i[None, None, :] >= p[:, None, None],
                  gamma[None, :, None] ** np.maximum(i[None, None, :] - p[:, None, None], 0), 0.0)
    ds = np.where((same & (p[None, :] >= p[:, None]))[:, None, :],
                  gamma[None, :, None] ** np.maximum(p[None, None, :] - p[:, None, None], 0), 0.0)
    decay = np.concatenate([dp.reshape(P, -1), ds.reshape(P, -1)], 1) * HD ** -0.5
    mb = np.zeros((P, P * (2 + NB)), np.float32)
    mb[:, 0:P] = np.eye(P)
    mb[:, P:2 * P] = np.where(p[None, :] <= p[:, None], 0.0, NEG)
    for b in range(NB):
        seen = (p[None, :] // NS == b) & (p[None, :] % NS <= p[:, None] % NS)
        mb[:, (2 + b) * P:(3 + b) * P] = np.where(seen, 0.0, NEG)
    return c, decay.astype(np.float32), mb


class Banks:

    def __init__(self, full, free):
        self.full, self.free = full, free
        self.n = [0] * 8
        self.jobs = {}
        self.per = None

    def job(self, key, bank):
        assert key not in self.jobs
        self.jobs[key] = (bank, self.n[bank], self.per)
        self.n[bank] += 1

    def loop(self, times, jobs):
        per = [0] * 8
        for _, bank in jobs:
            per[bank] += 1
        self.per = per
        for key, bank in jobs:
            self.job(key, bank)
        for b in range(8):
            self.n[b] += (times - 1) * per[b]
        self.per = None

    def count(self, key, l, it):
        bank, before, per = self.jobs[key]
        v = l * self.n[bank] + (before + 1)
        return v if per is None else v + it * per[bank]

    def bank(self, key):
        return self.jobs[key][0]

    def wait_room(self, eng, key, l, it=None):
        eng.wait_ge(self.free[self.bank(key)], self.count(key, l, it))

    def wait_full_before(self, eng, key, l, it=None):
        eng.wait_ge(self.full[self.bank(key)], self.count(key, l, it) - 1)

    def wait_full(self, eng, key, l, it=None):
        eng.wait_ge(self.full[self.bank(key)], self.count(key, l, it))

    def wait_taken(self, eng, key, l, it=None):
        eng.wait_ge(self.free[self.bank(key)], self.count(key, l, it) + 1)


    def wait_all_taken(self, eng, keys, l):
        last = {self.bank(key): key for key in sorted(keys, key=lambda key: self.jobs[key][1])}
        for key in last.values():
            self.wait_taken(eng, key, l)


def chunk_banks():
    return {0: (3, 4, 5, 6, 7), 1: (1, 0, 2, 3, 4), 2: (5, 6, 7, 2, 1), 3: (3, 4, 0, 5, 6), 4: (7, 1, 2, 3, 4)}


TURNS = {0: (0, 1), 1: (2, 3), 2: (4,)}
TURN_BANKS = {"rt": (5, 6, 7, 5, 6), "qT": (7, 2, 1, 7, 2), "kT": (0, 5, 6, 0, 5)}


def ret_units():
    return [(h, jb) for h in range(RH) for jb in range(TP)]


def fox_units():
    return [(h, qb) for h in range(FH) for qb in range(TP)]


D_BANKS = (4, 5, 6, 7, 4, 5, 6, 7, 4, 5)
U_BANKS = (6, 7, 4, 5)
STEPS = 3


def batch_jobs(tag, ahead, now):
    jobs = []
    if ahead is not None:
        jobs += [(("kt", tag, p), p % 2) for p in range(4)]
        jobs += [(("ss", tag), 2 + ahead), (("sn", tag), 4)]
    if now is not None:
        jobs += [(("pt", tag, 0), 6), (("pt", tag, 1), 7), (("so", tag), 5)]
    return jobs


def down_jobs(tag):
    return [(("d", tag, nc, t), D_BANKS[5 * nc + t]) for nc in range(2) for t in range(TT)]


def plan_banks(banks):
    j = banks.job
    for t in range(TT):
        for g in range(2):
            j(("hT", 0, t, g), (2 * t + g) % 3)
    cb = chunk_banks()

    def chunk(c):
        for t in range(TT):
            j(("c", c, t), cb[c][t])

    def turns(name):
        for t in range(TT):
            j((name, t), TURN_BANKS[name][t])

    chunk(0)
    j("taps", 1)
    j(("fl", 0), 0)
    j(("fl", 1), 2)
    chunk(1)
    turns("rt")
    j("flT", 7)
    for n, u in enumerate(ret_units()):
        j(("rs", u), n % 2)
        if n == 0:
            j(("ro", 0), 3)
            j(("ro", 1), 4)
    j("rst", 0)
    j("rss0", 1)
    j("rss1", 0)
    j("rds0", 1)
    j("rds1", 0)
    j("rso", 2)
    j("rsoT", 0)
    chunk(2)
    chunk(3)
    turns("qT")
    chunk(4)
    turns("kT")
    j("cs", 6)
    j("cc", 0)
    j("cn", 5)
    for n, k in enumerate(("cc_", "ch_", "cb_")):
        for i in range(4):
            j((k, i // 2, i % 2), ((7, 1, 2, 3), (4, 6, 5, 0))[n % 2][i])
    for n, (h, qb) in enumerate(fox_units()):
        j(("fs", h, qb), 4 + n % 3)
        j(("ft", h, qb), (7, 0)[n % 2])
        if h % 2 == 0 and qb == 0:
            j(("fo", h // 2), 1 + (h // 2) % 2)
    for g in range(3):
        j(("orT", g), 3 + g)
    for key, b in batch_jobs("pro", 0, None):
        j(key, b)
    banks.loop(STEPS, batch_jobs("b0", 1, 0) + batch_jobs("b1", 0, 1))
    for key, b in batch_jobs("p6", 1, 0) + batch_jobs("p7", None, 1):
        j(key, b)
    for n in range(2 * TT):
        j(("wo", n // TT, n % TT), n % 8)
    for t in range(TT):
        for g in range(2):
            j(("hT", 1, t, g), 4 + (2 * t + g) % 4)
    for i in range(4):
        j(("g", "pro", i // 2, i % 2), i)
    for i in range(4):
        j(("u", "pro", i // 2, i % 2), U_BANKS[i])
    banks.loop(PAIRS - 1, [(("g", "loop", i // 2, i % 2), i) for i in range(4)] + down_jobs("loop")
               + [(("u", "loop", i // 2, i % 2), U_BANKS[i]) for i in range(4)])
    for g in range(6):
        j(("last", g), g % 4)
    for key, b in down_jobs("end"):
        j(key, b)


def token_pieces(half):
    return [(0, HALF, 0)] if half == 0 else [(0, SEQ - HALF, HALF), (SEQ - HALF, HALF, None)]


def build(nc, a):
    with ExitStack() as ctx:
        sems = {}

        def sem(name):
            sems[name] = ctx.enter_context(nc.semaphore(name))
            return sems[name]

        bank = [ctx.enter_context(nc.psum_tensor(f"bank{i}", [P, 512], F32)) for i in range(8)]
        B = Banks([sem(f"full{i}") for i in range(8)], [sem(f"free{i}") for i in range(8)])
        plan_banks(B)

        base = (nc.sbuf_base + 31) // 32 * 32
        size = {F32: 4, F32R: 4, BF16: 2}
        top = [base]

        def at(name, shape, dt, offset):
            n = size[dt]
            for s in shape[1:]:
                n *= s
            return nc.alloc_sbuf_tensor_at(name, shape, dt, offset=offset), offset + (n + 31) // 32 * 32

        def own(name, shape, dt=F32):
            t, top[0] = at(name, shape, dt, top[0])
            return t

        def region(*groups):
            start, ends, out = top[0], [], []
            for g in groups:
                o = start
                for name, shape, dt in g:
                    t, o = at(name, shape, dt, o)
                    out.append(t)
                ends.append(o)
            top[0] = max(ends)
            return out

        const = own("const", [P, NCONST])

        def K(name):
            o, n = CONST[name]
            return const[:, o:o + n]

        maskb = own("maskb", [P, (2 + NB) * P], BF16)
        raw = own("raw", [P, SLOTS, 1024])
        whi = own("whi", [P, SLOTS, 1024], F32R)
        wlo = own("wlo", [P, SLOTS, 1024], F32R)
        x = own("x", [P, TT, D])
        hhi = own("hhi", [P, KT, NTOK], F32R)
        hlo = own("hlo", [P, KT, NTOK], F32R)
        taps = own("taps", [P, NCT, NTAP])
        last = own("last", [P, NCT, NLAST])
        sel = own("sel", [P, FH, P], F32R)
        ncp = own("ncp", [P, SEQ], F32R)
        ncn = own("ncn", [P, P], F32R)
        lf = own("lf", [P, TT, FH])
        lfx = own("lfx", [P, TP, 40])
        small = own("small", [P, 544])
        mhalf = own("mhalf", [P, 40])
        pst = own("pst", [P, 2, HD])
        ctot = own("ctot", [P, 1])
        wcn = own("wcn", [P, P])
        wcnh = own("wcnh", [P, P], F32R)
        fbias = own("fbias", [P, FH])
        ftap = own("ftap", [P, 2, 3])
        (fqg, fkg, gng, qbd) = region(
            [("fqg", [P, FW], F32), ("fkg", [P, FW], F32), ("gng", [P, RW], F32)],
            [("qbd", [P, 2, 640], F32)])
        (gains, os_, ncc) = region(
            [("gains", [P, D], F32)],
            [("os", [P, 4, P], F32), ("ncc", [P, PAST], F32R)])
        eb = own("eb", [P, 2, P], F32R)
        (fqT, fkT, fv, guhi, gulo, gact) = region(
            [("fqT", [P, 4, NTOK], F32), ("fkT", [P, 4, NTOK], F32), ("fv", [P, TT, FW], F32)],
            [("guhi", [P, 2, NTOK], F32R), ("gulo", [P, 2, NTOK], F32R), ("gact", [P, 2, NY], F32)])
        gs = own("gs", [P, TT, RW])
        (rT, kw, rv, decp, decs, s0, kb, kT, vb, rows, gpad, gu, _, lrows) = region(
            [("rT", [P, 4, NTOK], F32), ("kw", [P, TT, RW], F32), ("rv", [P, TT, RW], F32),
             ("decp", [P, RH, SEQ], F32), ("decs", [P, RH, P], F32), ("s0", [P, 2, NB * HD], F32)],
            [("kb", [P, 4, FW], F32), ("kT", [P, 4, PAST], F32), ("vb", [P, 2, 4, FW], F32)],
            [("rows", [NTAP, CW + DFF], F32)],
            [("gpad", [P, 2, PADDED], F32), ("gu", [P, 2, NTOK], F32), ("gap", [P, 512], F32),
             ("lrows", [NLAST, CW + DFF], F32)])
        (upad, ccs, flr, gnd, gnsq, lc, lcd, lexp, nct) = region(
            [("upad", [P, 2, PADDED], F32), ("ccs", [P, 2, NTOK], F32)],
            [("flr", [FH, NTOK], F32)],
            [("gnd", [P, TT * RH, HD], F32), ("gnsq", [P, TT * RH, HD], F32)],
            [("lc", [P, 4, 64], F32), ("lcd", [P, 4, 2, 64], F32), ("lexp", [P, P], F32),
             ("nct", [P, 512], F32R)])
        (xn, tA, n2, n1, ptr, vm, rso, qw, ycv, pf, pTf, ps, pTs) = region(
            [("xn", [P, 2, D], F32)],
            [("tA", [P, 2, 512], F32), ("n2", [P, 2, 512], F32), ("n1", [P, 512], F32)],
            [("ptr", [P, 3, 512], F32), ("vm", [P, 2, 512], F32), ("rso", [P, 2 * P], F32),
             ("qw", [P, 2, P], F32)],
            [("ycv", [P, 2, NY], F32)],
            [("pf", [P, 3, 512], F32), ("pTf", [P, 2, 512], F32)],
            [("ps", [P, 2, 640], F32), ("pTs", [P, 2, 640], F32)])

        oc = ccs

        SS, VAR, RS = 0, 8, 16
        FSS, FVAR, FRS = (32, 176), (80, 224), (128, 272)
        GS, GM, GQ, GV, GR = 320, 340, 360, 380, 400
        NM, RSUM, REC = 420, 452, 484
        SB = 516

        def col(c, n=1, rows_=P):
            return small[0:rows_, c:c + n]

        consts_in = sem("consts_in")
        masks_in = sem("masks_in")
        x_in = [sem(f"x_in{t}") for t in range(TT)]
        y_stored = sem("y_stored")
        pool_const = sem("pool_const")
        sel_ready = sem("sel_ready")
        raw_in = [sem(f"raw_in{i}") for i in range(SLOTS)]
        hi_split = sem("hi_split")
        lo_split = sem("lo_split")
        slab_used = sem("slab_used")
        rows_in = sem("rows_in")
        gains_in = sem("gains_in")
        foxg_in = sem("foxg_in")
        lc_in = sem("lc_in")
        dec_in = sem("dec_in")
        s0_in = sem("s0_in")
        k_in = sem("k_in")
        v_in = [sem(f"v_in{i}") for i in range(2)]
        x_done = sem("x_done")
        sumsq = sem("sumsq")
        rstd = sem("rstd")
        xn_ready = sem("xn_ready")
        h_hi = sem("h_hi")
        fl_z = sem("fl_z")
        fl_e = sem("fl_e")
        lf_ready = sem("lf_ready")
        lcd_ready = sem("lcd_ready")
        nct_ready = sem("nct_ready")
        nc_ready = sem("nc_ready")
        wcn_ready = sem("wcn_ready")
        lexp_ready = sem("lexp_ready")
        vm_used = sem("vm_used")
        rot_ready = sem("rot_ready")
        kw_ready = sem("kw_ready")
        silu_ready = sem("silu_ready")
        gs_ready = sem("gs_ready")
        qw_ready = sem("qw_ready")
        vm_ready = sem("vm_ready")
        s_new = sem("s_new")
        gn_d = sem("gn_d")
        gn_sq = sem("gn_sq")
        gn_v = sem("gn_v")
        gn_r = sem("gn_r")
        oret = sem("oret")
        fsq = sem("fsq")
        fss = sem("fss")
        frs = sem("frs")
        fn_ready = sem("fn_ready")
        k_stored = [sem(f"k_stored{i}") for i in range(2)]
        stores = sem("stores")
        hist_u = sem("hist_u")
        u_ready = sem("u_ready")
        cat_hi = sem("cat_hi")
        cat_lo = sem("cat_lo")
        nmax = sem("nmax")
        pnorm = sem("pnorm")
        q_ready = sem("q_ready")
        smax = sem("smax")
        snorm = sem("snorm")
        gpad_hist = sem("gpad_hist")
        gconv = sem("gconv")
        gsilu = sem("gsilu")
        gu_hi = sem("gu_hi")
        gu_ready = sem("gu_ready")
        glast = sem("glast")

        used_index = {}
        final = {}

        def mark(first, n, key):
            for s_ in range(first, first + n - 1):
                used_index[s_] = len(used_index)
            final[first + n - 1] = key

        mark(0, 4, ("c", 0, TT - 1))
        mark(FL, 2, ("fl", 1))
        for c in range(1, 5):
            mark(C0 + 4 * c, 4, ("c", c, TT - 1))
        for first, k in ((CC, "cc_"), (CH, "ch_"), (CB, "cb_")):
            mark(first, 2, (k, 1, 1))
        for n in range(2):
            mark(WO + 4 * n, 4, ("wo", n, 4))
        mark(G0, 2, ("g", "pro", 1, 1))
        mark(G0 + 2, 2, ("u", "pro", 1, 1))
        USED0 = len(used_index)
        USED = USED0 + 2 * (PAIRS - 1)
        STORES = 14
        HIS, CATS = 9, 2

        def wait_used(eng, n, l, it=None):
            if it is not None:
                j = n
                if j < 0:
                    assert j == -1
                    eng.wait_ge(B.full[B.bank(("d", "loop", 0, 1))], B.count(("d", "loop", 0, 1), l, it) - 1)
                elif j in (0, 4):
                    eng.wait_ge(slab_used, l * USED + it * 2 + (USED0 + 1 + j // 4))
                else:
                    key = {1: ("g", "loop", 1, 1), 2: ("d", "loop", 0, 4), 3: ("d", "loop", 1, 4)}[j]
                    B.wait_full(eng, key, l, it)
            elif n >= 0:
                if n in used_index:
                    eng.wait_ge(slab_used, l * USED + used_index[n] + 1)
                else:
                    B.wait_full(eng, final[n], l)

        def wait_k_stored(eng, t, l):
            half = t % 2
            eng.wait_ge(k_stored[half], l * (16 * ((TT + 1 - half) // 2)) + 16 * (t // 2 + 1))

        def slot(n):
            return n % SLOTS

        LPS = SLABS // SLOTS

        def wait_loaded(eng, n, l, it=None):
            v = l * (16 * LPS) + 16 * (n // SLOTS + 1)
            eng.wait_ge(raw_in[slot(n)], v if it is None else v + it * 32)

        def nth(n, l, it=None, more=1):
            v = l * SLABS + n + more
            return v if it is None else v + it * 6

        def width(n):
            return 4 * FH if n in (FL, FL + 1) else 1024

        parted = sem("parted")

        def apart(eng):
            eng.sem_inc(parted, 1)

        block = ctx.enter_context(nc.Block())

        def load_x(eng, t):
            src = a["x_prompt"][0, t * P:(t + 1) * P, :] if t < TP else a["x_sample"].rearrange("b s d -> (b s) d")
            eng.dma_start(x[:, t, :], src).then_inc(x_in[t], 16)

        @block.sync
        def _(sp):
            load_x(sp, 0)
            sp.dma_start(const[:, :], a["c_tables"]).then_inc(consts_in, 16)
            load_x(sp, 1)

            def w_tile(w, l, k, nk, c, n):
                return w[bass.ds(l, 1)].rearrange("o (k p) n -> p (o k) n", p=P)[:, k:k + nk, c:c + n]

            def load(n, l, src, it=None):
                sp.wait_ge(lo_split, nth(n, l, it, 1))
                apart(sp)
                dst = raw[:, slot(n), 0:width(n)].rearrange("p (k n) -> p k n", k=src.shape[1])
                sp.dma_start(dst, src).then_inc(raw_in[slot(n)], 16)

            def slab_src(n, l):
                w = a["w_in"]
                if n in (FL, FL + 1):
                    return w_tile(w, l, 4 * (n - FL), 4, COL_FL, FH)
                if n < CC:
                    c, i = divmod(n if n < FL else n - C0, 4)
                    return w_tile(w, l, 2 * i, 2, 512 * c, 512)
                if n < WO:
                    c, i = divmod(n - CC, 2)
                    return w_tile(w, l, 4 * i, 4, COL_CONV + CW * (1, 2, 0)[c], CW)
                if n < G0:
                    c, i = divmod(n - WO, 4)
                    return w_tile(a["w_out"], l, 2 * i, 2, 512 * c, 512)
                w, i = (a["w_gate"], n - G0) if n < G0 + 2 else (a["w_up"], n - G0 - 2)
                return w_tile(w, l, 4 * i, 4, 0, 256)

            def up_src(w, l, it, i):
                v = w[bass.ds(l, 1)].rearrange("o (k p) n -> p (o k) n", p=P)
                return v[:, 4 * i:4 * i + 4, bass.ds(it * 256 + 256, 256)]

            def down_src(l, it, c):
                v = a["w_down"][bass.ds(l, 1), bass.ds(it * 256, 256) if it is not None else
                                slice((PAIRS - 1) * 256, DFF), :]
                return v.rearrange("o (k p) n -> p (o k) n", p=P)[:, :, 512 * c:512 * c + 512]

            kview = a["cache_fox_k"].rearrange("l b (k p) h d -> (l b) p k (h d)", p=P)
            vview = a["cache_fox_v"].rearrange("l b (k p) h d -> (l b) p k (h d)", p=P)

            def load_k(l, b):
                sp.dma_start(kb[:, :, :], kview[bass.ds(l * NB + b, 1)].rearrange("o p k n -> p (o k) n"))\
                    .then_inc(k_in, 16)

            def load_v(l, b, u):
                sp.dma_start(vb[:, u], vview[bass.ds(l * NB + b, 1)].rearrange("o p k n -> p (o k) n"))\
                    .then_inc(v_in[u], 16)

            def first_loads(l, layer):
                sp.dma_start(gains[:, :], a["norm_mix"][bass.ds(layer, 1)].to_broadcast([P, D])).then_inc(gains_in, 16)
                for n in range(SLOTS):
                    load(n, l, slab_src(n, layer))

            first_loads(0, 0)
            with sp.Fori(0, DEPTH) as l:
                def one(name):
                    return a[name][bass.ds(l, 1)]

                sp.dma_start(fbias[:, :], one("fox_f_bias").to_broadcast([P, FH])).then_inc(foxg_in, 16)
                sp.dma_start(rows[0:16, 0:CW], one("state_conv").rearrange("o b w c -> (o b w) c")).then_inc(rows_in, 16)
                sp.dma_start(rows[0:16, CW:], one("state_ffn_conv").rearrange("o b w c -> (o b w) c")).then_inc(rows_in, 16)
                sp.dma_start(rows[16:19, 0:CW], one("conv_w").rearrange("o w c -> (o w) c")).then_inc(rows_in, 16)
                sp.dma_start(rows[16:19, CW:], one("ffn_conv_w").rearrange("o w c -> (o w) c")).then_inc(rows_in, 16)
                sp.dma_start(fqg[:, :], one("fox_q_gain").rearrange("o h d -> o (h d)").to_broadcast([P, FW])).then_inc(foxg_in, 16)
                sp.dma_start(fkg[:, :], one("fox_k_gain").rearrange("o h d -> o (h d)").to_broadcast([P, FW])).then_inc(foxg_in, 16)
                sp.dma_start(gng[:, :], one("ret_gn_gain").to_broadcast([P, RW])).then_inc(foxg_in, 16)
                sp.dma_start(decp[:, :, :], a["c_decay"][:, 0:RH * SEQ]).then_inc(dec_in, 16)
                sp.dma_start(decs[:, :, :], a["c_decay"][:, RH * SEQ:]).then_inc(dec_in, 16)
                for hp in range(2):
                    for par in range(2):
                        sp.dma_start(s0[64 * par:64 * par + 64, hp, :].rearrange("d (b e) -> d b e", b=NB),
                                     one("state_ret").rearrange("o b h d e -> h d (o b) e")[2 * hp + par])\
                            .then_inc(s0_in, 16)
                for n in range(3, 10):
                    load(n, l, slab_src(n, l))
                for n in range(10, 14):
                    load(n, l, slab_src(n, l))
                B.wait_taken(sp, "rst", l)
                for hp in range(2):
                    sp.dma_start(a["p_ret"][bass.ds(l, 1)].rearrange("o b h d e -> (o b h d) e")
                                 [P * hp:P * hp + P, :], pst[:, hp, :]).then_inc(stores, 16)
                sp.wait_ge(s_new, l + 1)
                for hp in range(2):
                    for par in range(2):
                        sp.dma_start(a["s_ret"][bass.ds(l, 1)].rearrange("o b h d e -> h d (o b) e")[2 * hp + par],
                                     s0[64 * par:64 * par + 64, hp, :].rearrange("d (b e) -> d b e", b=NB))\
                            .then_inc(stores, 16)
                for n in range(14, 18):
                    load(n, l, slab_src(n, l))
                sp.wait_ge(oret, l + 1)
                for blk in range(4):
                    sp.dma_start(lc[:, blk, :].rearrange("p (b h) -> p b h", b=NB),
                                 one("cache_fox_logf").rearrange("o b (k p) h -> k p (o b) h", p=P)[blk])\
                        .then_inc(lc_in, 16)
                for n in range(18, 23):
                    load(n, l, slab_src(n, l))
                sp.wait_ge(lf_ready, l + 1)
                sp.dma_start(a["p_fox_logf"][bass.ds(l, 1)].rearrange("o b (t p) h -> p (o b t) h", p=P),
                             lf[:, 0:TP, :]).then_inc(stores, 16)
                sp.dma_start(a["s_fox_logf"][bass.ds(l, 1)].rearrange("o b s h -> (o b s) h"),
                             lf[:, TS, :]).then_inc(stores, 16)
                for t in range(TT):
                    sp.wait_ge(fn_ready, l * (2 * TT) + TT + t + 1)
                    if t < TP:
                        dst = a["p_fox_k"][bass.ds(l, 1)].rearrange("o b s h d -> (o b s) (h d)")[t * P:(t + 1) * P, :]
                    else:
                        dst = a["s_fox_k"][bass.ds(l, 1)].rearrange("o b s h d -> (o b s) (h d)")
                    sp.dma_start(dst, n2[:, t % 2, :]).then_inc(k_stored[t % 2], 16)
                for n in range(23, 27):
                    load(n, l, slab_src(n, l))
                B.wait_taken(sp, ("c", 4, TT - 1), l)
                sp.dma_start(a["p_fox_v"][bass.ds(l, 1)].rearrange("o b (t p) h d -> p (o b t) (h d)", p=P),
                             fv[:, 0:TP, :]).then_inc(stores, 16)
                sp.dma_start(a["s_fox_v"][bass.ds(l, 1)].rearrange("o b s h d -> (o b s) (h d)"),
                             fv[:, TS, :]).then_inc(stores, 16)
                for n in range(27, 31):
                    load(n, l, slab_src(n, l))
                B.wait_full(sp, "rsoT", l)
                sp.wait_ge(stores, l * (16 * STORES) + 16 * 10)
                load_k(l, 0)
                load_v(l, 0, 0)
                load_v(l, 1, 1)
                B.wait_full(sp, ("kt", "pro", 3), l)
                load_k(l, 1)
                with sp.Fori(0, STEPS) as it:
                    for u in range(2):
                        B.wait_full(sp, ("kt", f"b{u}", 3), l, it)
                        load_k(l, it * 2 + (u + 2))
                        B.wait_full(sp, ("so", f"b{u}"), l, it)
                        load_v(l, it * 2 + (u + 2), u)
                sp.wait_ge(cat_lo, l * CATS + CATS)
                sp.dma_start(gains[:, :], one("norm_ffn").to_broadcast([P, D])).then_inc(gains_in, 16)
                for n in range(31, LOOP0):
                    load(n, l, slab_src(n, l))
                with sp.Fori(0, PAIRS - 1) as it:
                    for j in range(6):
                        src = (up_src(a["w_gate"], l, it, j) if j < 2 else down_src(l, it, j - 2) if j < 4
                               else up_src(a["w_up"], l, it, j - 4))
                        load(LOOP0 + j, l, src, it)
                for c in range(2):
                    load(DLAST + c, l, down_src(l, None, c))
                assert DEPTH == 2
                B.wait_full(sp, ("g", "loop", 1, 1), l, PAIRS - 2)
                apart(sp)
                first_loads(l + 1, DEPTH - 1 - l)
                for g in range(2, 6):
                    B.wait_taken(sp, ("last", g), l)
                    apart(sp)
                sp.wait_ge(gu_ready, l * PAIRS + PAIRS)
                apart(sp)
                for k_, (p_, s_), c0, c1 in ((0, ("p_conv", "s_conv"), 0, CW), (1, ("p_ffn", "s_ffn"), CW, CW + DFF)):
                    sp.dma_start(a[p_][bass.ds(l, 1)].rearrange("o b w c -> (o b w) c"), lrows[0:2, c0:c1]).then_inc(stores, 16)
                    sp.dma_start(a[s_][bass.ds(l, 1)].rearrange("o b w c -> (o b w) c"), lrows[2:18, c0:c1]).then_inc(stores, 16)
                sp.wait_ge(stores, l * (16 * STORES) + 16 * STORES)
                wait_k_stored(sp, TT - 2, l)
                wait_k_stored(sp, TT - 1, l)
                apart(sp)

            sp.wait_ge(x_done, 2 * TT * (DEPTH + 1))
            for t in range(TP):
                sp.dma_start(a["y_prompt"][0, t * P:(t + 1) * P, :], x[:, t, :]).then_inc(y_stored, 16)
            sp.dma_start(a["y_sample"].rearrange("b s d -> (b s) d"), x[:, TS, :]).then_inc(y_stored, 16)
            sp.wait_ge(y_stored, 16 * TT)
            sp.wait_ge(gains_in, 16 * (2 * DEPTH + 1))
            for s_ in range(SLOTS):
                sp.wait_ge(raw_in[s_], 16 * (LPS * DEPTH + 1))

        @block.gpsimd
        def _(pool):
            for b in range(8):
                pool.sem_inc(B.free[b], 1)
            pool.sem_inc(lo_split, SLOTS)
            pool.sem_inc(x_done, 2 * TT)
            pool.memset(mhalf[:, :], -0.5)
            pool.memset(lfx[:, :, :], 0.0)
            pool.memset(ncp[:, :].bitcast(F32), 0.0)
            pool.memset(small[:, :], 0.0)
            pool.drain().then_inc(pool_const, 1)
            pool.wait_ge(consts_in, 16)

            def rsqrt(ss, var, rs, n, scale, done):
                pool.tensor_scalar(col(var, n), col(ss, n), scale, EPS, ALU.mult, ALU.add)
                pool.drain()
                pool.tensor_tensor(col(rs, n), col(var, n), mhalf[:, 0:n], ALU.pow).then_inc(done, 1)

            def norm(which, l):
                for t in range(TT):
                    pool.wait_ge(sumsq, l * (2 * TT) + which * TT + t + 1)
                    apart(pool)
                    rsqrt(SS + t, VAR + t, RS + t, 1, 1.0 / D, rstd)

            with pool.Fori(0, DEPTH) as l:
                norm(0, l)
                pool.wait_ge(foxg_in, l * 64 + 64)
                apart(pool)
                pool.tensor_scalar(fqg[:, :], fqg[:, :], HD ** -0.5, None, ALU.mult)
                for t in range(TT):
                    pool.wait_ge(rot_ready, l * TT + t + 1)
                    if t == 0:
                        B.wait_full(pool, "taps", l)
                    pool.tensor_tensor(kw[:, t, :].rearrange("p (h d) -> p h d", h=RH),
                                       n2[:, t % 2, 256:512].rearrange("p (h d) -> p h d", h=RH),
                                       K("kdec").rearrange("p (t h) -> p t h", t=TT)[:, t, :].unsqueeze(2).to_broadcast([P, RH, HD]),
                                       ALU.mult).then_inc(kw_ready, 1)
                for t in range(TT):
                    pool.wait_ge(silu_ready, l * TT + t + 1)
                    pool.tensor_tensor(gs[:, t, :], gs[:, t, :], gng[:, :], ALU.mult)
                pool.drain().then_inc(gs_ready, 1)
                pool.wait_ge(gn_v, l + 1)
                apart(pool)
                rsqrt(GV, GQ, GR, TT * RH, 1.0 / HD, gn_r)
                for t in range(TT):
                    pool.wait_ge(fss, l * (2 * TT) + t + 1)
                    apart(pool)
                    rsqrt(FSS[0] + 8 * t, FVAR[0] + 8 * t, FRS[0] + 8 * t, FH, 1.0 / HD, frs)
                pool.wait_ge(lc_in, l * 64 + 64)
                apart(pool)
                pool.tensor_copy(lcd[:, :, 0, :], lc[:, :, :])
                pool.tensor_copy(lcd[:, :, 1, :], lc[:, :, :])
                pool.drain().then_inc(lcd_ready, 1)
                for t in range(TT):
                    pool.wait_ge(fss, l * (2 * TT) + TT + t + 1)
                    apart(pool)
                    rsqrt(FSS[1] + 8 * t, FVAR[1] + 8 * t, FRS[1] + 8 * t, FH, 1.0 / HD, frs)
                pool.wait_ge(nc_ready, l + 1)
                B.wait_taken(pool, "taps", l)
                apart(pool)
                pool.memset(upad[:, :, 0:2], 0.0)
                for ft in range(2):
                    pool.tensor_copy(upad[:, ft, 2 + SEQ:].rearrange("p (b s) -> p b s", b=NB)[:, :, 0:2],
                                     taps[:, ft, 0:16].rearrange("p (b w) -> p b w", b=NB))
                pool.drain().then_inc(hist_u, 1)
                pool.wait_ge(u_ready, l + 1)
                apart(pool)
                for ft in range(2):
                    pool.tensor_copy(last[:, ft, 0:2], upad[:, ft, SEQ:SEQ + 2])
                    pool.tensor_copy(last[:, ft, 2:18].rearrange("p (b w) -> p b w", b=NB),
                                     upad[:, ft, 2 + SEQ:].rearrange("p (b s) -> p b s", b=NB)[:, :, NS:NS + 2])

                def queries(b, u):
                    for par in range(2):
                        dst = qbd[64 * par:64 * par + 64, u, :].rearrange("p (c s) -> p c s", c=4)[:, :, 16 * par:16 * par + 16]
                        src = fqT[64 * par:64 * par + 64, :, SEQ:][:, :, bass.ds(b * 16, 16)]
                        pool.tensor_copy(dst, src)
                        pool.drain()
                    pool.tensor_tensor(eb[:, u, :], K("e0"), K("bsel")[:, bass.ds(b, 1)].to_broadcast([P, P]), ALU.mult)
                    pool.drain().then_inc(q_ready, 1)

                pool.wait_ge(fn_ready, l * (2 * TT) + 2 * TT)
                B.wait_taken(pool, ("qT", TT - 1), l)
                apart(pool)
                pool.memset(qbd[:, :, :], 0.0)
                pool.drain()
                B.wait_taken(pool, ("fs", FH - 1, TP - 1), l)
                apart(pool)
                queries(0, 0)
                with pool.Fori(0, STEPS) as it:
                    for u in range(2):
                        B.wait_full_before(pool, ("sn", f"b{u}"), l, it)
                        apart(pool)
                        queries(it * 2 + (u + 1), 1 - u)
                B.wait_full(pool, ("sn", "b0"), l, STEPS - 1)
                apart(pool)
                queries(NB - 1, 1)

                norm(1, l)
                pool.wait_ge(cat_lo, l * CATS + CATS)
                apart(pool)
                pool.memset(gpad[:, :, 0:2], 0.0)

                def ffn_pads(c):
                    for f in range(2):
                        tp = taps[:, bass.ds(c + f, 1), :] if not isinstance(c, int) else taps[:, c + f:c + f + 1, :]
                        pool.tensor_copy(gpad[:, f, 2 + SEQ:].rearrange("p (b s) -> p b s", b=NB)[:, :, 0:2],
                                         tp[:, 0, 0:16].rearrange("p (b w) -> p b w", b=NB))
                        pool.tensor_copy(ftap[:, f:f + 1, :], tp[:, :, 16:19])
                    pool.drain().then_inc(gpad_hist, 1)

                def ffn_last(c):
                    for f in range(2):
                        lp = last[:, bass.ds(c + f, 1), :] if not isinstance(c, int) else last[:, c + f:c + f + 1, :]
                        pool.tensor_copy(lp[:, 0, 0:2], gpad[:, f, SEQ:SEQ + 2])
                        pool.tensor_copy(lp[:, 0, 2:18].rearrange("p (b w) -> p b w", b=NB),
                                         gpad[:, f, 2 + SEQ:].rearrange("p (b s) -> p b s", b=NB)[:, :, NS:NS + 2])
                    pool.drain().then_inc(glast, 1)

                ffn_pads(2)
                pool.wait_ge(gconv, l * (2 * PAIRS) + 2)
                apart(pool)
                ffn_last(2)
                with pool.Fori(0, PAIRS - 1) as it:
                    ffn_pads(it * 2 + 4)
                    pool.wait_ge(gconv, l * (2 * PAIRS) + it * 2 + 4)
                    apart(pool)
                    ffn_last(it * 2 + 4)

        @block.scalar
        def _(act):
            split_to = [0]

            def split(n, l, it=None):
                wait_loaded(act, n, l, it)
                act.activation(whi[:, slot(n), 0:width(n)], raw[:, slot(n), 0:width(n)], ACT.Copy).then_inc(hi_split, 1)

            def upto(n, l):
                while split_to[0] <= n:
                    wait_used(act, split_to[0] - SLOTS, l)
                    split(split_to[0], l)
                    split_to[0] += 1

            def split_loop(j, l, it):
                wait_used(act, j - SLOTS, l, it)
                split(LOOP0 + j, l, it)

            def norm(which, l, splits):
                for t in range(TT + 1):
                    if t < TT:
                        act.wait_ge(x_in[t], 16)
                        act.wait_ge(x_done, l * (2 * TT) + (which * TT + TT + t + 1))
                        if t >= 2:
                            B.wait_full(act, ("hT", which, t - 2, 1), l)
                        act.activation(xn[:, t % 2, :], x[:, t, :], ACT.Square, accum_out=col(SS + t)).then_inc(sumsq, 1)
                    if t > 0:
                        for g in range(2):
                            B.wait_full(act, ("hT", which, t - 1, g), l)
                            act.activation(hhi[:, 4 * g:4 * g + 4, (t - 1) * P:t * P],
                                           bank[B.bank(("hT", which, t - 1, g))][:, :].rearrange("p (k n) -> p k n", k=4),
                                           ACT.Copy).then_inc(h_hi, 1)
                    if t in splits:
                        upto(splits[t], l)

            act.wait_ge(x_in[0], 16)
            for t in range(2, TT):
                load_x(act, t)
            act.dma_start(maskb[:, :], a["c_masks"]).then_inc(masks_in, 16)
            act.wait_ge(pool_const, 1)
            with act.Fori(0, DEPTH) as l:
                split_to[0] = 0

                def evac(key, out, l, it=None, view=None):
                    B.wait_full(act, key, l, it)
                    src = bank[B.bank(key)][:, :] if view is None else view(bank[B.bank(key)])
                    act.activation(out, src, ACT.Copy).then_inc(B.free[B.bank(key)], 1)

                def quad(b):
                    return b[:, :].rearrange("p (c n) -> p c n", c=4)

                norm(0, l, {0: 1, 1: 2})
                upto(FL + 1, l)
                evac("taps", taps[:, :, :], l, view=lambda b: b[:, 0:NCT * NTAP].rearrange("p (c n) -> p c n", c=NCT))
                upto(C0 + 4, l)
                for half in range(2):
                    evac(("fl", half), flr[:, half * HALF:(half + 1) * HALF], l, view=lambda b: b[0:FH, 0:HALF])
                upto(C0 + 6, l)

                def turned(name, dst, n, l):
                    for t in range(TT):
                        evac((name, t), dst[:, :, t * P:(t + 1) * P], l, view=quad)
                        if t in (1, 3):
                            upto(n + t - 1, l)

                turned("rt", rT, C0 + 7, l)
                for t in range(TT):
                    B.wait_full(act, ("c", 1, t), l)
                    bk = bank[B.bank(("c", 1, t))]
                    act.activation(gs[:, t, :], bk[:, 256:512], ACT.Silu).then_inc(silu_ready, 1)
                    act.activation(rv[:, t, :], bk[:, 0:256], ACT.Copy).then_inc(B.free[B.bank(("c", 1, t))], 1)
                upto(C0 + 10, l)
                evac("rst", pst[:, :, :], l, view=lambda b: b[:, 0:2 * HD].rearrange("p (c n) -> p c n", c=2))
                evac("rso", rso[:, :], l, view=lambda b: b[:, 0:2 * P])
                upto(C0 + 11, l)
                act.wait_ge(gn_d, l + 1)
                act.activation(gnsq[:, :, :], gnd[:, :, :], ACT.Square).then_inc(gn_sq, 1)
                for c in (2, 3):
                    k_ = C0 + 4 * c + 3
                    upto(k_ + 2, l)
                    for t in range(TT):
                        B.wait_full(act, ("c", c, t), l)
                        n_ = (c - 2) * TT + t
                        if n_ >= 2:
                            act.wait_ge(fss, l * (2 * TT) + (n_ - 1))
                        act.activation(tA[:, t % 2, :], bank[B.bank(("c", c, t))][:, :], ACT.Square).then_inc(fsq, 1)
                        if t == 1:
                            upto(k_ + 3, l)
                    turned(*(("qT", fqT) if c == 2 else ("kT", fkT)), k_ + 4, l)
                    if c == 2:
                        act.wait_ge(fl_z, l * 2 + 1)
                        act.activation(n1[:, 80:120], n1[:, 40:80], ACT.Exp, scale=-1.0).then_inc(fl_e, 1)
                        act.wait_ge(fl_z, l * 2 + 2)
                        act.activation(n1[:, 160:200], n1[:, 120:160], ACT.Ln).then_inc(fl_e, 1)
                k_ = C0 + 19
                for t in range(TT):
                    evac(("c", 4, t), fv[:, t, :], l)
                    if t == 1:
                        upto(k_ + 3, l)
                act.wait_ge(oret, l + 1)
                for key, dst, r_, r0 in (("cs", ncp, 8, 32), ("cc", ncc, 64, 64)):
                    B.wait_full(act, key, l)
                    bk = bank[B.bank(key)]
                    act.activation(dst[0:r_, :], bk[0:r_, :], ACT.Copy, scale=-1.0)
                    act.activation(nct[r0:r0 + r_, :], bk[r0:r0 + r_, :], ACT.Copy, scale=-1.0).then_inc(nct_ready, 1)
                act.wait_ge(wcn_ready, l + 1)
                act.activation(ncn[0:64, :], wcn[0:64, :], ACT.Copy)
                act.activation(wcnh[64:128, :], wcn[64:128, :], ACT.Copy).then_inc(nct_ready, 1)
                upto(k_ + 4, l)
                act.wait_ge(nc_ready, l + 1)
                for i in range(4):
                    ft, half = i // 2, i % 2
                    evac(("cc_", ft, half), ccs[:, ft, half * HALF:(half + 1) * HALF], l, view=lambda b: b[:, 0:HALF])
                upto(WO - 1, l)
                units = fox_units()
                NU = len(units)
                for n in range(NU + 3):
                    if n < NU:
                        h, qb = units[n]
                        N = P * (qb + 1)
                        key = ("fs", h, qb)
                        if n == 3:
                            B.wait_taken(act, ("cb_", 1, 1), l)
                            act.activation(hhi[:, 6:8, :], oc[:, :, :], ACT.Copy).then_inc(cat_hi, 1)
                        if n in (6, 10, 14):
                            upto(WO + (n - 6) // 4, l)
                        act.wait_ge(nmax, l * NU + n + 1)
                        act.activation(pf[:, n % 3, 0:N], bank[B.bank(key)][:, 0:N], ACT.Exp, bias=col(NM + n),
                                       accum_out=col(RSUM + n)).then_inc(B.free[B.bank(key)], 1)
                    if 2 <= n < NU + 2:
                        h, qb = units[n - 2]
                        N = P * (qb + 1)
                        evac(("ft", h, qb), pTf[:, n % 2, 0:N], l, view=lambda b: b[:, 0:N])
                    if n >= 3:
                        h, qb = units[n - 3]
                        if h % 2 and qb == TP - 1:
                            key = ("fo", h // 2)
                            B.wait_full(act, key, l)
                            act.activation(hhi[:, 2 + h // 2, 0:SEQ], bank[B.bank(key)][:, :], ACT.Copy).then_inc(cat_hi, 1)
                for g in range(3):
                    w_ = 256 if g < 2 else P
                    B.wait_full(act, ("orT", g), l)
                    act.activation(hhi[:, 0:2, 256 * g:256 * g + w_],
                                   bank[B.bank(("orT", g))][:, :].rearrange("p (r c) -> p r c", r=2)[:, :, 0:w_],
                                   ACT.Copy).then_inc(cat_hi, 1)

                def step(tag, ahead, now, nb, it=None):
                    if ahead is not None:
                        for p_ in (0, 2):
                            evac(("kt", tag, p_), kT[:, p_, :], l, it)
                    if now is not None:
                        evac(("pt", tag, 0), pTs[:, now, 0:512], l, it)
                    if ahead is not None:
                        act.wait_ge(smax, nb)
                        o = SB + 8 * ahead
                        for key, c0, n_, acc in ((("ss", tag), 0, 512, 3), (("sn", tag), 512, P, 4)):
                            act.activation(ps[:, ahead, c0:c0 + n_], bank[B.bank(key)][:, 0:n_], ACT.Exp, bias=col(o + 2),
                                           accum_out=col(o + acc)).then_inc(B.free[B.bank(key)], 1)

                step("pro", 0, None, l * NB + 1)
                with act.Fori(0, STEPS) as it:
                    step("b0", 1, 0, l * NB + it * 2 + 2, it)
                    step("b1", 0, 1, l * NB + it * 2 + 3, it)
                step("p6", 1, 0, l * NB + NB)
                step("p7", None, 1, None)
                B.wait_taken(act, ("so", "p7"), l)
                act.activation(hhi[:, 2:6, SEQ:], os_[:, :, :], ACT.Copy).then_inc(cat_hi, 1)

                upto(G0 + 1, l)
                norm(1, l, {1: G0 + 2})

                def gate(tag, it=None):
                    for i in range(4):
                        ft, half = i // 2, i % 2
                        key = ("g", tag, ft, half)
                        B.wait_full(act, key, l, it)
                        for c0, c1, t0 in token_pieces(half):
                            src = bank[B.bank(key)][:, c0:c1]
                            if t0 is None:
                                ins = act.activation(gpad[:, ft, 2 + SEQ:].rearrange("p (b s) -> p b s", b=NB)[:, :, 2:],
                                                     src.rearrange("p (b s) -> p b s", b=NB), ACT.Copy)
                            else:
                                ins = act.activation(gpad[:, ft, 2 + t0:2 + t0 + c1 - c0], src, ACT.Copy)
                        ins.then_inc(B.free[B.bank(key)], 1)

                def silu(done, tiles=(0, 1)):
                    for ft in tiles:
                        act.wait_ge(gconv, done + ft + 1)
                        act.activation(gact[:, ft, :], gact[:, ft, :], ACT.Silu).then_inc(gsilu, 1)

                gate("pro")
                upto(G0 + 4, l)
                silu(l * (2 * PAIRS))
                upto(G0 + 5, l)
                with act.Fori(0, PAIRS - 1) as it:
                    split_loop(2, l, it)
                    B.wait_room(act, ("d", "loop", 0, 1), l, it)
                    act.activation(guhi[:, :, :], gu[:, :, :], ACT.Copy).then_inc(gu_hi, 1)
                    split_loop(3, l, it)
                    act.wait_ge(glast, l * PAIRS + it + 1)
                    gate("loop", it)
                    split_loop(4, l, it)
                    silu(l * (2 * PAIRS) + it * 2 + 2, [0])
                    split_loop(5, l, it)
                    silu(l * (2 * PAIRS) + it * 2 + 2, [1])
                    for j in (6, 7):
                        split_loop(j, l, it)
                B.wait_room(act, ("d", "end", 0, 1), l)
                act.activation(guhi[:, :, :], gu[:, :, :], ACT.Copy).then_inc(gu_hi, 1)
                for g in range(6):
                    B.wait_full(act, ("last", g), l)
                    act.activation(lrows[:, g * 512:(g + 1) * 512], bank[B.bank(("last", g))][0:NLAST, :],
                                   ACT.Copy).then_inc(B.free[B.bank(("last", g))], 1)
                B.wait_full(act, ("d", "end", 1, 4), l)

        @block.vector
        def _(dve):
            split_to = [0]

            def split(n, l, it=None):
                dve.wait_ge(hi_split, nth(n, l, it))
                s_, w_ = slot(n), width(n)
                dve.tensor_tensor(wlo[:, s_, 0:w_], raw[:, s_, 0:w_], whi[:, s_, 0:w_].bitcast(F32),
                                  ALU.subtract).then_inc(lo_split, 1)

            def upto(n, l):
                while split_to[0] <= n:
                    split(split_to[0], l)
                    split_to[0] += 1

            def lo(out, full_, hi):
                return dve.tensor_tensor(out, full_, hi.bitcast(F32), ALU.subtract)

            def norm(which, l, splits, before=lambda t: None):
                for t in range(TT + 1):
                    before(t)
                    if t < TT:
                        if t == 0:
                            dve.wait_ge(gains_in, l * 32 + 16 * (which + 1))
                        dve.wait_ge(rstd, l * (2 * TT) + which * TT + t + 1)
                        dve.scalar_tensor_tensor(out=xn[:, t % 2, :], in0=x[:, t, :], scalar=col(RS + t), in1=gains[:, :],
                                                 op0=ALU.mult, op1=ALU.mult).then_inc(xn_ready, 1)
                    if t > 0:
                        for g in range(2):
                            key = ("hT", which, t - 1, g)
                            dve.wait_ge(h_hi, l * (4 * TT) + which * (2 * TT) + 2 * (t - 1) + g + 1)
                            lo(hlo[:, 4 * g:4 * g + 4, (t - 1) * P:t * P],
                               bank[B.bank(key)][:, :].rearrange("p (k n) -> p k n", k=4),
                               hhi[:, 4 * g:4 * g + 4, (t - 1) * P:t * P]).then_inc(B.free[B.bank(key)], 1)
                    if t in splits:
                        upto(splits[t], l)

            def heads(ap, n=FH):
                return ap.rearrange("p (h d) -> p h d", h=n)

            dve.wait_ge(consts_in, 16)
            dve.wait_ge(pool_const, 1)
            ident = K("ident")
            dve.tensor_tensor(small[:, 536:544], ident[:, 0:8], ident[:, 32:40], ALU.add)
            dve.drain()
            dve.tensor_copy(sel[:, :, :], small[:, 536:544].unsqueeze(2).to_broadcast([P, FH, P])).then_inc(sel_ready, 1)
            with dve.Fori(0, DEPTH) as l:
                split_to[0] = 0
                norm(0, l, {0: 1, 1: 2})
                upto(C0 + 5, l)
                cs = K("cs").rearrange("p (t s d) -> p t s d", t=TT, s=2)
                for t in range(TT):
                    key = ("c", 0, t)
                    dve.drain()
                    B.wait_full(dve, key, l)
                    bk = bank[B.bank(key)]
                    xh = bk[:, :].rearrange("p (h s d) -> p h s d", h=8, s=2)
                    ta = tA[:, 0, :]
                    tb = tA[:, 1, :].rearrange("p (h s d) -> p h s d", h=8, s=2)
                    cos = cs[:, t, 0, :].unsqueeze(1)
                    sin = cs[:, t, 1, :].unsqueeze(1)
                    dve.tensor_tensor(ta.rearrange("p (h d) -> p h d", h=16), bk[:, :].rearrange("p (h d) -> p h d", h=16),
                                      cos.to_broadcast([P, 16, 32]), ALU.mult)
                    dve.tensor_tensor(tb[:, :, 0, :], xh[:, :, 1, :], sin.to_broadcast([P, 8, 32]), ALU.mult)
                    dve.tensor_tensor(tb[:, :, 1, :], xh[:, :, 0, :], sin.to_broadcast([P, 8, 32]),
                                      ALU.mult).then_inc(B.free[B.bank(key)], 1)
                    dve.drain()
                    if t >= 2:
                        dve.wait_ge(kw_ready, l * TT + t - 1)
                        B.wait_full(dve, ("rt", t - 2), l)
                    tav = ta.rearrange("p (h s d) -> p h s d", h=8, s=2)
                    nv = n2[:, t % 2, :].rearrange("p (h s d) -> p h s d", h=8, s=2)
                    dve.tensor_tensor(nv[:, :, 0, :], tav[:, :, 0, :], tb[:, :, 0, :], ALU.subtract)
                    dve.tensor_tensor(nv[:, :, 1, :], tav[:, :, 1, :], tb[:, :, 1, :], ALU.add).then_inc(rot_ready, 1)
                    if t in (0, 3):
                        upto(C0 + 6 + t // 3, l)

                upto(C0 + 10, l)
                dve.wait_ge(dec_in, l * 32 + 32)
                dve.wait_ge(kw_ready, l * TT + TT)
                B.wait_full(dve, "flT", l)
                dve.wait_ge(foxg_in, l * 64 + 64)
                dve.tensor_tensor(lf[:, :, :], bank[B.bank("flT")][:, 0:40].rearrange("p (t h) -> p t h", t=TT),
                                  fbias[:, :].unsqueeze(1).to_broadcast([P, TT, FH]), ALU.add).then_inc(B.free[B.bank("flT")], 1)
                for n, (h, jb) in enumerate(ret_units()):
                    N = SEQ - P * jb
                    key = ("rs", (h, jb))
                    B.wait_full(dve, key, l)
                    dve.tensor_tensor(ptr[:, n % 3, 0:N], bank[B.bank(key)][:, 0:N], decp[:, h, 0:N],
                                      ALU.mult).then_inc(B.free[B.bank(key)], 1)
                dve.tensor_tensor(qw[:, :, :], rT[:, 0:2, SEQ:], K("qdec").rearrange("p (c n) -> p c n", c=2),
                                  ALU.mult).then_inc(qw_ready, 1)
                for par in range(2):
                    key = f"rss{par}"
                    B.wait_full(dve, key, l)
                    dve.tensor_tensor(ptr[:, 1, :].rearrange("p (c r n) -> p c r n", c=2, r=2)[:, :, par, :],
                                      bank[B.bank(key)][:, 0:2 * P].rearrange("p (c n) -> p c n", c=2),
                                      decs[:, :, :].rearrange("p (c r) n -> p c r n", r=2)[:, :, par, :],
                                      ALU.mult).then_inc(B.free[B.bank(key)], 1)
                for h in range(RH):
                    if h == 2:
                        dve.wait_ge(vm_used, l * 2 + 1)
                    if h == 3:
                        B.wait_full(dve, "rds0", l)
                    dve.tensor_tensor(vm[:, h % 2, :].rearrange("p (b e) -> p b e", b=NB),
                                      rv[:, TS, h * HD:(h + 1) * HD].unsqueeze(1).to_broadcast([P, NB, HD]),
                                      K("bmask")[:, 0:NB].unsqueeze(2).to_broadcast([P, NB, HD]),
                                      ALU.mult).then_inc(vm_ready, 1)
                B.wait_full(dve, "rso", l)
                for hp in range(2):
                    key = f"rds{hp}"
                    dve.scalar_tensor_tensor(out=s0[:, hp, :], in0=s0[:, hp, :], scalar=K("g16")[:, hp:hp + 1],
                                             in1=bank[B.bank(key)][:, :], op0=ALU.mult,
                                             op1=ALU.add).then_inc(B.free[B.bank(key)], 1)
                dve.drain().then_inc(s_new, 1)
                srcs = ((("ro", 0), 0, 8), (("ro", 1), 8, 8), ("rsoT", 16, 4))

                def group(key, n):
                    return bank[B.bank(key)][:, 0:n * HD].rearrange("p (g d) -> p g d", g=n)

                for key, g0, n in srcs:
                    B.wait_full(dve, key, l)
                    dve.tensor_reduce(col(GS + g0, n), group(key, n), X, ALU.add)
                dve.drain()
                dve.tensor_scalar(col(GM, 20), col(GS, 20), 1.0 / HD, None, ALU.mult)
                dve.drain()
                for key, g0, n in srcs:
                    dve.tensor_tensor(gnd[:, g0:g0 + n, :], group(key, n),
                                      col(GM + g0, n).unsqueeze(2).to_broadcast([P, n, HD]),
                                      ALU.subtract).then_inc(B.free[B.bank(key)], 1)
                dve.drain().then_inc(gn_d, 1)
                upto(C0 + 11, l)
                dve.wait_ge(gn_sq, l + 1)
                dve.tensor_reduce(col(GV, 20), gnsq[:, :, :], X, ALU.add).then_inc(gn_v, 1)
                upto(C0 + 12, l)
                dve.wait_ge(gn_r, l + 1)
                dve.tensor_tensor(gnsq[:, :, :], gnd[:, :, :], col(GR, 20).unsqueeze(2).to_broadcast([P, 20, HD]), ALU.mult)
                dve.drain()
                dve.wait_ge(gs_ready, l + 1)
                dve.tensor_tensor(gs[:, :, :].rearrange("p t c -> p (t c)"), gnsq[:, :, :].rearrange("p g d -> p (g d)"),
                                  gs[:, :, :].rearrange("p t c -> p (t c)"), ALU.mult).then_inc(oret, 1)

                for c in (2, 3):
                    i = c - 2
                    k_ = C0 + 4 * c + 3
                    upto(k_ + 2, l)
                    gain = fqg if c == 2 else fkg
                    for t in range(TT + 1):
                        if t < TT:
                            dve.wait_ge(fsq, l * (2 * TT) + i * TT + t + 1)
                            dve.tensor_reduce(col(FSS[i] + 8 * t, 8), heads(tA[:, t % 2, :]), X, ALU.add).then_inc(fss, 1)
                        if t > 0:
                            s_ = t - 1
                            key = ("c", c, s_)
                            dve.drain()
                            dve.wait_ge(frs, l * (2 * TT) + i * TT + s_ + 1)
                            dve.tensor_tensor(heads(n1[:, :]), heads(bank[B.bank(key)][:, :]),
                                              col(FRS[i] + 8 * s_, 8).unsqueeze(2).to_broadcast([P, FH, HD]),
                                              ALU.mult).then_inc(B.free[B.bank(key)], 1)
                            dve.drain()
                            if s_ >= 2:
                                B.wait_full(dve, ("qT" if c == 2 else "kT", s_ - 2), l)
                                if c == 3:
                                    wait_k_stored(dve, s_ - 2, l)
                            elif s_ == 0:
                                if c == 2:
                                    dve.wait_ge(kw_ready, l * TT + TT)
                                else:
                                    B.wait_full(dve, ("qT", TT - 1), l)
                            dve.tensor_tensor(n2[:, s_ % 2, :], n1[:, :], gain[:, :], ALU.mult).then_inc(fn_ready, 1)
                        if t == 2:
                            upto(k_ + 3, l)
                    upto(k_ + 6, l)
                    if c == 2:
                        _, az, e, u_, lnu, d_, r_, q_, w_, o_ = (n1[:, 40 * i:40 * i + 40] for i in range(10))
                        z = lf[:, :, :].rearrange("p t h -> p (t h)")
                        dve.drain()
                        dve.scalar_tensor_tensor(out=az, in0=z, scalar=-1.0, in1=z, op0=ALU.mult, op1=ALU.max).then_inc(fl_z, 1)
                        dve.wait_ge(fl_e, l * 2 + 1)
                        dve.tensor_scalar(u_, e, 1.0, None, ALU.add).then_inc(fl_z, 1)
                        dve.drain()
                        dve.tensor_scalar(d_, u_, -1.0, 1e-30, ALU.add, ALU.max)
                        dve.tensor_scalar(o_, u_, 1.0, None, ALU.is_equal)
                        dve.drain()
                        dve.reciprocal(r_, d_)
                        dve.drain()
                        dve.tensor_tensor(q_, e, r_, ALU.mult)
                        dve.tensor_tensor(w_, o_, e, ALU.mult)
                        dve.drain()
                        dve.wait_ge(fl_e, l * 2 + 2)
                        dve.tensor_tensor(q_, lnu, q_, ALU.mult)
                        dve.drain()
                        dve.tensor_tensor(q_, q_, w_, ALU.add)
                        dve.drain()
                        dve.scalar_tensor_tensor(out=lf[:, :, :].rearrange("p t h -> p (t h)"), in0=z, scalar=0.0, in1=q_,
                                                 op0=ALU.min, op1=ALU.subtract)
                        dve.drain()
                        dve.tensor_copy(lfx[:, :, 0:8], lf[:, 0:TP, :])
                        dve.tensor_copy(lfx[:, :, 32:40], lf[:, 0:TP, :])
                        dve.drain().then_inc(lf_ready, 1)
                        dve.tensor_tensor(lexp[:, :].rearrange("p (b h) -> p b h", h=FH),
                                          lf[:, TS, :].unsqueeze(1).to_broadcast([P, 16, FH]),
                                          K("bmask").unsqueeze(2).to_broadcast([P, 16, FH]), ALU.mult).then_inc(lexp_ready, 1)
                upto(C0 + 19 + 3, l)
                dve.wait_ge(nct_ready, l * 3 + 1)
                dve.scalar_tensor_tensor(out=ncp[32:40, :], in0=bank[B.bank("cs")][32:40, :], scalar=-1.0,
                                         in1=nct[32:40, :].bitcast(F32), op0=ALU.mult,
                                         op1=ALU.subtract).then_inc(B.free[B.bank("cs")], 1)
                dve.wait_ge(nct_ready, l * 3 + 2)
                dve.tensor_copy(ctot[:, :], bank[B.bank("cc")][:, PAST - 1:PAST])
                dve.scalar_tensor_tensor(out=ncc[64:128, :], in0=bank[B.bank("cc")][64:128, :], scalar=-1.0,
                                         in1=nct[64:128, :].bitcast(F32), op0=ALU.mult,
                                         op1=ALU.subtract).then_inc(B.free[B.bank("cc")], 1)
                dve.drain()
                B.wait_full(dve, "cn", l)
                dve.tensor_scalar(wcn[:, :], bank[B.bank("cn")][:, 0:P], ctot[:, 0:1], -1.0, ALU.add,
                                  ALU.mult).then_inc(B.free[B.bank("cn")], 1)
                dve.drain().then_inc(wcn_ready, 1)
                dve.wait_ge(nct_ready, l * 3 + 3)
                lo(ncn[64:128, :], wcn[64:128, :], wcnh[64:128, :]).then_inc(nc_ready, 1)
                upto(C0 + 19 + 4, l)

                def by_batch(ap):
                    return ap.rearrange("p (b s) -> p b s", b=NB)

                def mul_bank(out_of, key, other):
                    ft, half = key[-2:]
                    for c0, c1, t0 in token_pieces(half):
                        src = bank[B.bank(key)][:, c0:c1]
                        t1 = None if t0 is None else t0 + c1 - c0
                        ins = dve.tensor_tensor(out_of(ft, t0, t1), by_batch(src) if t0 is None else src, other(ft, t0, t1),
                                                ALU.mult)
                    return ins

                def plain(buf):
                    return lambda ft, t0, t1: by_batch(buf[:, ft, SEQ:]) if t0 is None else buf[:, ft, t0:t1]

                def in_padded(buf):
                    return lambda ft, t0, t1: (by_batch(buf[:, ft, 2 + SEQ:])[:, :, 2:] if t0 is None
                                               else buf[:, ft, 2 + t0:2 + t1])

                def conv_out(buf):
                    return lambda ft, t0, t1: (by_batch(buf[:, ft, NY - NB * (NS + 2):NY])[:, :, 2:] if t0 is None
                                               else buf[:, ft, t0:t1])

                def conv(out, u, ft, tap):
                    ins = dve.tensor_scalar(out[:, ft, 0:NY], u[:, ft, 0:NY], tap(0), None, ALU.mult)
                    for j in (1, 2):
                        dve.drain()
                        ins = dve.scalar_tensor_tensor(out=out[:, ft, :], in0=u[:, ft, j:j + NY], scalar=tap(j),
                                                       in1=out[:, ft, :], op0=ALU.mult, op1=ALU.add)
                    return ins

                dve.wait_ge(hist_u, l + 1)
                wait_k_stored(dve, TT - 2, l)
                wait_k_stored(dve, TT - 1, l)
                for i in range(4):
                    key = ("ch_", i // 2, i % 2)
                    B.wait_full(dve, key, l)
                    B.wait_taken(dve, ("cc_", i // 2, i % 2), l)
                    mul_bank(in_padded(upad), key, plain(ccs)).then_inc(B.free[B.bank(key)], 1)
                dve.drain().then_inc(u_ready, 1)
                upto(CH + 3, l)
                B.wait_taken(dve, "taps", l)
                for ft in range(2):
                    conv(ycv, upad, ft, lambda j: taps[:, ft, 16 + j:17 + j])
                dve.drain()
                for i in range(4):
                    key = ("cb_", i // 2, i % 2)
                    B.wait_full(dve, key, l)
                    mul_bank(plain(oc), key, conv_out(ycv)).then_inc(B.free[B.bank(key)], 1)
                units = fox_units()
                NU = len(units)
                for n in range(NU + 4):
                    if n < NU:
                        h, qb = units[n]
                        B.wait_full(dve, ("fs", h, qb), l)
                        if n == 4:
                            dve.wait_ge(cat_hi, l * HIS + 1)
                            lo(hlo[:, 6:8, :], oc[:, :, :], hhi[:, 6:8, :]).then_inc(cat_lo, 1)
                        if n in (8, 12, 16):
                            upto(WO + n // 4 - 2, l)
                        dve.tensor_reduce(col(NM + n), bank[B.bank(("fs", h, qb))][:, 0:P * (qb + 1)], X, ALU.max,
                                          negate=True).then_inc(nmax, 1)
                    if 1 <= n < NU + 1:
                        m = n - 1
                        h, qb = units[m]
                        N = P * (qb + 1)
                        B.wait_taken(dve, ("fs", h, qb), l)
                        dve.reciprocal(col(REC + m), col(RSUM + m))
                        dve.drain()
                        dve.tensor_scalar(pf[:, m % 3, 0:N], pf[:, m % 3, 0:N], col(REC + m), None, ALU.mult).then_inc(pnorm, 1)
                    if n >= 4:
                        h, qb = units[n - 4]
                        if h % 2 and qb == TP - 1:
                            key = ("fo", h // 2)
                            dve.wait_ge(cat_hi, l * HIS + 2 + h // 2)
                            lo(hlo[:, 2 + h // 2, 0:SEQ], bank[B.bank(key)][:, :],
                               hhi[:, 2 + h // 2, 0:SEQ]).then_inc(B.free[B.bank(key)], 1)
                for g in range(3):
                    w_ = 256 if g < 2 else P
                    key = ("orT", g)
                    dve.wait_ge(cat_hi, l * HIS + 6 + g)
                    lo(hlo[:, 0:2, 256 * g:256 * g + w_], bank[B.bank(key)][:, :].rearrange("p (r c) -> p r c", r=2)[:, :, 0:w_],
                       hhi[:, 0:2, 256 * g:256 * g + w_]).then_inc(B.free[B.bank(key)], 1)

                def step(tag, ahead, now, b, it=None):
                    if ahead is not None:
                        for p_ in (1, 3):
                            key = ("kt", tag, p_)
                            B.wait_full(dve, key, l, it)
                            dve.tensor_copy(kT[:, p_, :], bank[B.bank(key)][:, :]).then_inc(B.free[B.bank(key)], 1)
                    if now is not None:
                        key = ("pt", tag, 1)
                        B.wait_full(dve, key, l, it)
                        dve.tensor_copy(pTs[:, now, 512:640], bank[B.bank(key)][:, 0:P]).then_inc(B.free[B.bank(key)], 1)
                    if ahead is not None:
                        o = SB + 8 * ahead
                        for key, n_, c_ in ((("ss", tag), 512, 0), (("sn", tag), P, 1)):
                            B.wait_full(dve, key, l, it)
                            dve.tensor_reduce(col(o + c_), bank[B.bank(key)][:, 0:n_], X, ALU.max, negate=True)
                        dve.drain()
                        dve.tensor_tensor(col(o + 2), col(o), col(o + 1), ALU.min).then_inc(smax, 1)
                        B.wait_taken(dve, ("ss", tag), l, it)
                        B.wait_taken(dve, ("sn", tag), l, it)
                        dve.tensor_tensor(col(o + 5), col(o + 3), col(o + 4), ALU.add)
                        dve.drain()
                        dve.reciprocal(col(o + 6), col(o + 5))
                        dve.drain()
                        dve.tensor_scalar(ps[:, ahead, :], ps[:, ahead, :], col(o + 6), None, ALU.mult).then_inc(snorm, 1)
                    if now is not None:
                        key = ("so", tag)
                        B.wait_full(dve, key, l, it)
                        for par in range(2):
                            src = bank[B.bank(key)][64 * par:64 * par + 64, 0:P].rearrange("p (c s) -> p c s", c=4)
                            ins = dve.tensor_copy(os_[64 * par:64 * par + 64, :, bass.ds(b * 16, 16)],
                                                  src[:, :, 16 * par:16 * par + 16])
                        ins.then_inc(B.free[B.bank(key)], 1)

                step("pro", 0, None, 0)
                with dve.Fori(0, STEPS) as it:
                    step("b0", 1, 0, it * 2, it)
                    step("b1", 0, 1, it * 2 + 1, it)
                step("p6", 1, 0, 6)
                step("p7", None, 1, 7)
                dve.drain()
                dve.wait_ge(cat_hi, l * HIS + HIS)
                lo(hlo[:, 2:6, SEQ:], os_[:, :, :], hhi[:, 2:6, SEQ:]).then_inc(cat_lo, 1)

                def add(key, c, t, it=None):
                    B.wait_full(dve, key, l, it)
                    dve.tensor_tensor(x[:, t, 512 * c:512 * c + 512], x[:, t, 512 * c:512 * c + 512],
                                      bank[B.bank(key)][:, :], ALU.add).then_inc(B.free[B.bank(key)], 1)

                for c in range(2):
                    upto(WO + 4 * c + 5, l)
                    for t in range(TT if c == 0 else 0):
                        add(("wo", c, t), c, t)
                        if t == 1:
                            upto(WO + 6, l)

                def complete(t):
                    for t_ in (0, 1) if t == 0 else range(t + 1, min(t + 2, TT)):
                        add(("wo", 1, t_), 1, t_)
                        dve.drain().then_inc(x_done, 1)

                norm(1, l, {1: G0 + 2}, complete)
                upto(G0 + 3, l)

                def gate_conv(tag, ft, it=None):
                    if ft == 0:
                        dve.drain()
                        for i in range(4):
                            B.wait_taken(dve, ("g", tag, i // 2, i % 2), l, it)
                        dve.wait_ge(gpad_hist, l * PAIRS + 1 if it is None else l * PAIRS + it + 2)
                    conv(gact, gpad, ft, lambda j: ftap[:, ft, j:j + 1]).then_inc(gconv, 1)

                def product(wait, done):
                    dve.drain()
                    dve.wait_ge(gsilu, done)
                    for i in range(4):
                        wait(i)
                        mul_bank(plain(gu), ("u", "pro", i // 2, i % 2), conv_out(gact)).then_inc(B.free[U_BANKS[i]], 1)

                gate_conv("pro", 0)
                upto(G0 + 4, l)
                gate_conv("pro", 1)
                upto(G0 + 5, l)
                with dve.Fori(0, PAIRS - 1) as it:
                    product(lambda i: B.wait_full_before(dve, ("d", "loop", 0, U_BANKS[i] - 4), l, it),
                            l * (2 * PAIRS) + it * 2 + 2)
                    split(LOOP0 + 2, l, it)
                    dve.wait_ge(gu_hi, l * PAIRS + it + 1)
                    lo(gulo[:, :, :], gu[:, :, :], guhi[:, :, :]).then_inc(gu_ready, 1)
                    split(LOOP0 + 3, l, it)
                    gate_conv("loop", 0, it)
                    split(LOOP0 + 4, l, it)
                    for n in range(2 * TT):
                        add(("d", "loop", n // TT, n % TT), n // TT, n % TT, it)
                        if n == 4:
                            split(LOOP0 + 5, l, it)
                    dve.drain()
                    gate_conv("loop", 1, it)
                    split(LOOP0 + 6, l, it)
                    split(LOOP0 + 7, l, it)
                product(lambda i: B.wait_full_before(dve, ("d", "end", 0, U_BANKS[i] - 4), l),
                        l * (2 * PAIRS) + 2 * PAIRS)
                dve.wait_ge(gu_hi, l * PAIRS + PAIRS)
                lo(gulo[:, :, :], gu[:, :, :], guhi[:, :, :]).then_inc(gu_ready, 1)
                for n in range(2 * TT):
                    add(("d", "end", n // TT, n % TT), n // TT, n % TT)
                    if n >= TT:
                        dve.drain().then_inc(x_done, 1)

        @block.tensor
        def _(pe):
            ident = K("ident")
            identb = maskb[:, 0:P]

            def mm(out, lhsT, rhs, start, stop):
                return pe.matmul(out, lhsT=lhsT, rhs=rhs, start=start, stop=stop, skip_group_check=True)

            def mm3(out, lh, ll, rh, rl, start, stop):
                mm(out, lh, rh, start, False)
                mm(out, lh, rl, False, False)
                return mm(out, ll, rh, False, stop)

            def fill(ins, key):
                ins.then_inc(B.full[B.bank(key)], 1)

            def ready(n, l, it=None):
                pe.wait_ge(lo_split, nth(n, l, it, SLOTS + 1))

            def wait_h(which, l, t):
                for g in range(2):
                    B.wait_taken(pe, ("hT", which, t, g), l)

            def tm_slab(n, i, last_, acts, nk, kbase, keys, l, it=None, tiles=range(TT)):
                ready(n, l, it)
                s_ = slot(n)
                hi, lo_ = acts
                for t in tiles:
                    out = bank[B.bank(keys[t])][:, :]
                    if i == 0:
                        B.wait_room(pe, keys[t], l, it)
                    for k in range(nk):
                        ts = slice(t * P, t * P + P)
                        ins = mm3(out, hi[:, kbase + k, ts], lo_[:, kbase + k, ts], whi[:, s_, 512 * k:512 * k + 512],
                                  wlo[:, s_, 512 * k:512 * k + 512], i == 0 and k == 0, last_ and k == nk - 1)
                    if last_:
                        fill(ins, keys[t])
                if not last_ and t == TT - 1:
                    ins.then_inc(slab_used, 1)

            def fm_job(n0, keys, l, it=None, parts=(0, 1)):
                for i in parts:
                    ready(n0 + i, l, it)
                    s_ = slot(n0 + i)
                    for key in keys:
                        ft, half = key[-2:]
                        out = bank[B.bank(key)][:, 0:HALF]
                        if i == 0:
                            B.wait_room(pe, key, l, it)
                        for k in range(4):
                            ws = slice(256 * k + P * ft, 256 * k + P * ft + P)
                            ts = slice(half * HALF, half * HALF + HALF)
                            ins = mm3(out, whi[:, s_, ws], wlo[:, s_, ws], hhi[:, 4 * i + k, ts], hlo[:, 4 * i + k, ts],
                                      i == 0 and k == 0, i == 1 and k == 3)
                        if i == 1:
                            fill(ins, key)
                    if i == 0 and half == 1:
                        ins.then_inc(slab_used, 1)

            def transposes(key, parts, l, it=None):
                B.wait_room(pe, key, l, it)
                if parts[0][1].shape[0] < P:
                    apart(pe)
                for dst, src in parts:
                    ins = pe.transpose(dst, src, ident[0:src.shape[0], 0:src.shape[0]])
                fill(ins, key)

            def norm(which, l, after):
                for t in range(TT):
                    pe.wait_ge(xn_ready, l * (2 * TT) + which * TT + t + 1)
                    for g in range(2):
                        key = ("hT", which, t, g)
                        bk = bank[B.bank(key)]
                        transposes(key, [(bk[:, k * P:k * P + P], xn[:, t % 2, (4 * g + k) * P:(4 * g + k + 1) * P])
                                         for k in range(4)], l)
                    after(t)

            def turn(name, src, t, l):
                key = (name, t)
                bk = bank[B.bank(key)]
                transposes(key, [(bk[:, k * P:k * P + P], src[:, k * P:k * P + P]) for k in range(4)], l)

            def chunk0(i, l, tiles=range(TT)):
                tm_slab(i, i, i == 3, (hhi, hlo), 2, 2 * i, [("c", 0, t) for t in range(TT)], l, tiles=tiles)

            def chunk(c, l, name, ready_):
                for i, tiles in ((0, range(3)), (1, range(3)), (0, range(3, TT)), (1, range(3, TT)), (2, range(TT)), (3, range(TT))):
                    tm_slab(C0 + 4 * c + i, i, i == 3, (hhi, hlo), 2, 2 * i, [("c", c, t) for t in range(TT)], l, tiles=tiles)
                    if TS in tiles:
                        for t in TURNS.get(i, ()):
                            ready_(t)
                            turn(name, n2[:, t % 2, :], t, l)

            pe.wait_ge(consts_in, 16)
            pe.wait_ge(pool_const, 1)
            pe.wait_ge(sel_ready, 1)
            with pe.Fori(0, DEPTH) as l:
                def first_slabs(t):
                    if t > 0:
                        wait_h(0, l, t - 1)
                        for i in range(2):
                            chunk0(i, l, [t - 1])

                norm(0, l, first_slabs)
                first_slabs(TT)
                for i in (2, 3):
                    chunk0(i, l)
                pe.wait_ge(rows_in, l * 64 + 64)
                transposes("taps", [(bank[B.bank("taps")][:, c * NTAP:(c + 1) * NTAP], rows[:, c * P:(c + 1) * P])
                                    for c in range(NCT)], l)
                for i in range(2):
                    ready(FL + i, l)
                    s_ = slot(FL + i)
                    for half in range(2):
                        key = ("fl", half)
                        if i == 0:
                            B.wait_room(pe, key, l)
                        for k in range(4):
                            ws = slice(k * FH, k * FH + FH)
                            ts = slice(half * HALF, half * HALF + HALF)
                            ins = mm3(bank[B.bank(key)][0:FH, 0:HALF], whi[:, s_, ws], wlo[:, s_, ws], hhi[:, 4 * i + k, ts],
                                      hlo[:, 4 * i + k, ts], i == 0 and k == 0, i == 1 and k == 3)
                        if i == 1:
                            fill(ins, key)
                    if i == 0:
                        ins.then_inc(slab_used, 1)
                chunk(1, l, "rt", lambda t: pe.wait_ge(rot_ready, l * TT + t + 1))
                for half in range(2):
                    B.wait_taken(pe, ("fl", half), l)
                transposes("flT", [(bank[B.bank("flT")][:, t * FH:(t + 1) * FH], flr[:, t * P:(t + 1) * P])
                                   for t in range(TT)], l)

                B.wait_all_taken(pe, [("rt", t) for t in range(TT)] + [("c", 1, t) for t in range(TT)], l)
                units = ret_units()
                pieces = iter([(i, t) for i in range(3) for t in range(3)])

                def chunk2(i, tiles, l):
                    tm_slab(C0 + 8 + i, i, i == 3, (hhi, hlo), 2, 2 * i, [("c", 2, t) for t in range(TT)], l, tiles=tiles)

                def piece(l):
                    i, t = next(pieces)
                    chunk2(i, [t], l)

                for n in range(len(units) + 1):
                    if n % 2 == 0 and 0 < n <= 12:
                        piece(l)
                    if n < len(units):
                        h, jb = units[n]
                        r0 = 64 * (h % 2)
                        key = ("rs", (h, jb))
                        B.wait_room(pe, key, l)
                        fill(mm(bank[B.bank(key)][:, 0:SEQ - P * jb], rT[r0:r0 + 64, 2 + h // 2, jb * P:jb * P + P],
                                rT[r0:r0 + 64, h // 2, jb * P:SEQ], True, True), key)
                    if n > 0:
                        m = n - 1
                        h, jb = units[m]
                        B.wait_taken(pe, ("rs", (h, jb)), l)
                        if m == 0:
                            B.wait_room(pe, ("ro", 0), l)
                            B.wait_room(pe, ("ro", 1), l)
                        for ib in range(jb, TP):
                            c0 = (ib % 2) * 256 + h * HD
                            key = ("ro", ib // 2)
                            ins = mm(bank[B.bank(key)][:, c0:c0 + HD], ptr[:, m % 3, (ib - jb) * P:(ib - jb + 1) * P],
                                     rv[:, jb, h * HD:(h + 1) * HD], m == 0 and ib % 2 == 0, h == RH - 1 and ib == jb)
                            if h == RH - 1 and ib == jb and ib % 2:
                                fill(ins, key)
                pe.wait_ge(kw_ready, l * TT + TT)
                B.wait_room(pe, "rst", l)
                for h in range(RH):
                    r0 = 64 * (h % 2)
                    for t in range(TP):
                        ins = mm(bank[B.bank("rst")][r0:r0 + 64, (h // 2) * HD:(h // 2 + 1) * HD], kw[:, t, h * HD:(h + 1) * HD],
                                 rv[:, t, h * HD:(h + 1) * HD], t == 0, t == TP - 1)
                fill(ins, "rst")
                piece(l)
                for par in range(2):
                    r0 = 64 * par
                    key = f"rss{par}"
                    B.wait_room(pe, key, l)
                    for hp in range(2):
                        ins = mm(bank[B.bank(key)][:, hp * P:(hp + 1) * P], rT[r0:r0 + 64, 2 + hp, SEQ:],
                                 rT[r0:r0 + 64, hp, SEQ:], True, True)
                    fill(ins, key)
                piece(l)
                for h in range(RH):
                    r0 = 64 * (h % 2)
                    key = f"rds{h // 2}"
                    pe.wait_ge(vm_ready, l * RH + h + 1)
                    if h % 2 == 0:
                        B.wait_room(pe, key, l)
                    ins = mm(bank[B.bank(key)][r0:r0 + 64, :], kw[:, TS, h * HD:(h + 1) * HD], vm[:, h % 2, :], True, True)
                    if h % 2 == 0:
                        ins.then_inc(vm_used, 1)
                    else:
                        fill(ins, key)
                piece(l)
                pe.wait_ge(qw_ready, l + 1)
                pe.wait_ge(s0_in, l * 64 + 64)
                for par in range(2):
                    B.wait_taken(pe, f"rss{par}", l)
                B.wait_room(pe, "rso", l)
                for h in range(RH):
                    r0 = 64 * (h % 2)
                    out = bank[B.bank("rso")]
                    c0 = (h // 2) * P
                    mm(out[r0:r0 + 64, c0:c0 + P], rv[:, TS, h * HD:(h + 1) * HD], ptr[:, 1, h * P:(h + 1) * P], h < 2, False)
                    for b in range(NB):
                        ins = mm(out[r0:r0 + 64, c0 + b * NS:c0 + (b + 1) * NS], s0[r0:r0 + 64, h // 2, b * HD:(b + 1) * HD],
                                 qw[r0:r0 + 64, h // 2, b * NS:(b + 1) * NS], False, b == NB - 1)
                fill(ins, "rso")
                chunk2(0, [3], l)
                B.wait_taken(pe, "rso", l)
                transposes("rsoT", [(bank[B.bank("rsoT")][:, hp * P:(hp + 1) * P], rso[:, hp * P:(hp + 1) * P])
                                    for hp in range(2)], l)

                chunk2(0, [TS], l)
                for i in (1, 2):
                    chunk2(i, [3, TS], l)
                chunk2(3, range(TT), l)
                chunk(3, l, "qT", lambda t: pe.wait_ge(fn_ready, l * (2 * TT) + t + 1))
                chunk(4, l, "kT", lambda t: pe.wait_ge(fn_ready, l * (2 * TT) + TT + t + 1))
                pe.wait_ge(lf_ready, l + 1)
                B.wait_room(pe, "cs", l)
                for i in range(TP):
                    ins = mm(bank[B.bank("cs")][0:40, P * i:], lfx[:, i, :], K("tri")[:, 384:896 - P * i], i == 0, i == TP - 1)
                fill(ins, "cs")
                pe.wait_ge(lcd_ready, l + 1)
                B.wait_room(pe, "cc", l)
                for i in range(TP):
                    ins = mm(bank[B.bank("cc")][:, P * i:], lcd[:, i, :, :].rearrange("p a b -> p (a b)"),
                             K("tri")[:, 384:896 - P * i], i == 0, i == TP - 1)
                fill(ins, "cc")
                pe.wait_ge(lexp_ready, l + 1)
                B.wait_room(pe, "cn", l)
                fill(mm(bank[B.bank("cn")][:, 0:P], lexp[:, :], K("tris"), True, True), "cn")
                for first, name in ((CC, "cc_"), (CH, "ch_"), (CB, "cb_")):
                    fm_job(first, [(name, i // 2, i % 2) for i in range(4)], l)

                pe.wait_ge(masks_in, 16)
                pe.wait_ge(nc_ready, l + 1)
                B.wait_all_taken(pe, [(name, t) for name in ("qT", "kT") for t in range(TT)]
                                 + [("c", 4, t) for t in range(TT)], l)
                units = fox_units()
                NU = len(units)
                for n in range(NU + 3):
                    if n < NU:
                        h, qb = units[n]
                        r0, N = 64 * (h % 2), P * (qb + 1)
                        key = ("fs", h, qb)
                        out = bank[B.bank(key)]
                        B.wait_room(pe, key, l)
                        mm(out[:, 0:N], fqT[r0:r0 + 64, h // 2, qb * P:(qb + 1) * P], fkT[r0:r0 + 64, h // 2, 0:N], True, False)
                        mm(out[:, 0:N], sel[:, h, :], ncp[:, 0:N], False, False)
                        fill(mm(out[:, N - P:N], identb, maskb[:, P:2 * P], False, True), key)
                    if 2 <= n < NU + 2:
                        m = n - 2
                        h, qb = units[m]
                        key = ("ft", h, qb)
                        pe.wait_ge(pnorm, l * NU + m + 1)
                        bk = bank[B.bank(key)]
                        transposes(key, [(bk[:, k * P:(k + 1) * P], pf[:, m % 3, k * P:(k + 1) * P]) for k in range(qb + 1)], l)
                    if n >= 3:
                        m = n - 3
                        h, qb = units[m]
                        r0 = 64 * (h % 2)
                        key = ("fo", h // 2)
                        B.wait_taken(pe, ("ft", h, qb), l)
                        if h % 2 == 0 and qb == 0:
                            B.wait_room(pe, key, l)
                        for k in range(qb + 1):
                            ins = mm(bank[B.bank(key)][r0:r0 + 64, qb * P:(qb + 1) * P], fv[:, k, h * HD:(h + 1) * HD],
                                     pTf[:, m % 2, k * P:(k + 1) * P], k == 0, k == qb)
                        if h % 2 and qb == TP - 1:
                            fill(ins, key)
                pe.wait_ge(oret, l + 1)
                for g in range(3):
                    bk = bank[B.bank(("orT", g))]
                    transposes(("orT", g), [(bk[:, r * 256 + (t % 2) * P:r * 256 + (t % 2) * P + P], gs[:, t, r * P:(r + 1) * P])
                                            for t in range(2 * g, min(2 * g + 2, TT)) for r in range(2)], l)

                def step(tag, ahead, now, b, it=None):
                    nb = b if ahead is None else b - 1
                    if ahead is not None:
                        pe.wait_ge(k_in, (l * NB + b + 1) * 16)
                        for p_ in range(4):
                            key = ("kt", tag, p_)
                            bk = bank[B.bank(key)]
                            transposes(key, [(bk[:, k * P:(k + 1) * P], kb[:, k, p_ * P:(p_ + 1) * P]) for k in range(4)], l, it)
                    if now is not None:
                        pe.wait_ge(snorm, l * NB + nb + 1)
                        for g, ks in enumerate((range(4), range(4, 5))):
                            key = ("pt", tag, g)
                            bk = bank[B.bank(key)]
                            transposes(key, [(bk[:, (k % 4) * P:(k % 4 + 1) * P], ps[:, now, k * P:(k + 1) * P]) for k in ks], l, it)
                    if ahead is not None:
                        pe.wait_ge(q_ready, l * NB + b + 1)
                        for p_ in (2, 3):
                            B.wait_taken(pe, ("kt", tag, p_), l, it)
                        for name, keys_, sums, n_ in (("ss", lambda p_: kT[:, p_, :], ncc[:, :], PAST),
                                                      ("sn", lambda p_: fkT[:, p_, SEQ:], ncn[:, :], P)):
                            key = (name, tag)
                            out = bank[B.bank(key)][:, 0:n_]
                            B.wait_room(pe, key, l, it)
                            for p_ in range(4):
                                mm(out, qbd[:, ahead, p_ * P:(p_ + 1) * P], keys_(p_), p_ == 0, False)
                            ins = mm(out, eb[:, ahead, :], sums, False, name == "ss")
                            if name == "sn":
                                ins = mm(out, identb, maskb[:, bass.ds(b * P + 2 * P, P)], False, True)
                            fill(ins, key)
                    if now is not None:
                        pe.wait_ge(v_in[now], l * 64 + ((nb // 2 + 1) * 16 if it is None else it * 16 + 16))
                        B.wait_taken(pe, ("pt", tag, 0), l, it)
                        B.wait_taken(pe, ("pt", tag, 1), l, it)
                        key = ("so", tag)
                        B.wait_room(pe, key, l, it)
                        for p_ in range(4):
                            for k in range(5):
                                v = vb[:, now, k, p_ * P:(p_ + 1) * P] if k < 4 else fv[:, TS, p_ * P:(p_ + 1) * P]
                                ins = mm(bank[B.bank(key)][:, p_ * 32:(p_ + 1) * 32], v,
                                         pTs[:, now, k * P + 32 * p_:k * P + 32 * p_ + 32], k == 0, k == 4)
                        fill(ins, key)

                step("pro", 0, None, 0)
                with pe.Fori(0, STEPS) as it:
                    step("b0", 1, 0, it * 2 + 1, it)
                    step("b1", 0, 1, it * 2 + 2, it)
                step("p6", 1, 0, NB - 1)
                def out_slab(n, l, tiles=range(TT)):
                    c, i = divmod(n, 4)
                    tm_slab(WO + n, i, i == 3, (hhi, hlo), 2, 2 * i, [("wo", c, t) for t in range(TT)], l, tiles=tiles)

                pe.wait_ge(cat_lo, l * CATS + 1)
                B.wait_all_taken(pe, [("fo", p_) for p_ in range(4)] + [("orT", g) for g in range(3)], l)
                for n in range(SLOTS - 1):
                    out_slab(n, l, range(TP))
                step("p7", None, 1, NB - 1)
                out_slab(SLOTS - 1, l, range(TP))
                pe.wait_ge(cat_lo, l * CATS + CATS)
                for n in range(SLOTS):
                    out_slab(n, l, [TS])
                for n in range(SLOTS, 8):
                    out_slab(n, l)

                def gate_part(i, half):
                    fm_job(G0, [("g", "pro", ft, half) for ft in range(2)], l, parts=(i,))

                def first_half(t):
                    if t == TP - 1:
                        for t_ in range(TP - 1):
                            wait_h(1, l, t_)
                    if t >= TP - 1:
                        gate_part(t - (TP - 1), 0)

                norm(1, l, first_half)
                for t in (TP - 1, TS):
                    wait_h(1, l, t)
                for i in range(2):
                    gate_part(i, 1)
                fm_job(G0 + 2, [("u", "pro", i // 2, i % 2) for i in range(4)], l)

                def down(first, tag, it=None):
                    for c in range(2):
                        tm_slab(first + c, 0, True, (guhi, gulo), 2, 0, [("d", tag, c, t) for t in range(TT)], l, it)

                with pe.Fori(0, PAIRS - 1) as it:
                    fm_job(LOOP0, [("g", "loop", i // 2, i % 2) for i in range(4)], l, it)
                    pe.wait_ge(gu_ready, l * PAIRS + it + 1)
                    down(LOOP0 + 2, "loop", it)
                    fm_job(LOOP0 + 4, [("u", "loop", i // 2, i % 2) for i in range(4)], l, it)
                pe.wait_ge(glast, l * PAIRS + PAIRS)
                for g in range(6):
                    bk = bank[B.bank(("last", g))]
                    transposes(("last", g), [(bk[0:NLAST, k * P:(k + 1) * P], last[:, 4 * g + k, :]) for k in range(4)], l)
                pe.wait_ge(gu_ready, l * PAIRS + PAIRS)
                down(DLAST, "end")


INS = ("x_prompt", "x_sample", "cache_fox_k", "cache_fox_v", "cache_fox_logf", "state_ret", "state_conv",
       "state_ffn_conv", "norm_mix", "w_in", "ret_gn_gain", "fox_q_gain", "fox_k_gain", "fox_f_bias", "conv_w",
       "w_out", "norm_ffn", "w_gate", "w_up", "ffn_conv_w", "w_down")
OUTS = (("y_prompt", (1, SEQ, D)), ("y_sample", (NB, NS, D)),
        ("p_fox_k", (DEPTH, 1, SEQ, FH, HD)), ("p_fox_v", (DEPTH, 1, SEQ, FH, HD)), ("p_fox_logf", (DEPTH, 1, SEQ, FH)),
        ("p_ret", (DEPTH, 1, RH, HD, HD)), ("p_conv", (DEPTH, 1, 2, CW)), ("p_ffn", (DEPTH, 1, 2, DFF)),
        ("s_fox_k", (DEPTH, NB, NS, FH, HD)), ("s_fox_v", (DEPTH, NB, NS, FH, HD)), ("s_fox_logf", (DEPTH, NB, NS, FH)),
        ("s_ret", (DEPTH, NB, RH, HD, HD)), ("s_conv", (DEPTH, NB, 2, CW)), ("s_ffn", (DEPTH, NB, 2, DFF)))


def kernel(**inputs):
    import ml_dtypes
    from concourse import bacc
    from concourse.bass_utils import run_bass_kernel_spmd

    nc = bacc.Bacc("TRN2", target_bir_lowering=False, num_devices=1, dynamic_dma_scratch_size=1024)
    c_tables, c_decay, c_masks = tables()
    arrays = {name: np.ascontiguousarray(inputs[name]) for name in INS}
    arrays.update(c_tables=c_tables, c_decay=c_decay, c_masks=c_masks.astype(ml_dtypes.bfloat16))
    types = {"c_masks": BF16}
    a = {name: nc.dram_tensor("in_" + name, list(v.shape), types.get(name, F32), kind="ExternalInput").ap()
         for name, v in arrays.items()}
    for name, shape in OUTS:
        a[name] = nc.dram_tensor("out_" + name, list(shape), F32, kind="ExternalOutput").ap()
    build(nc, a)
    res = run_bass_kernel_spmd(nc, [{"in_" + name: v for name, v in arrays.items()}], core_ids=[0])
    return tuple(res.results[0]["out_" + name] for name, _ in OUTS)
```
